# Optimizing a Trainium2 kernel written in Bass

```python
import functools
import jax, jax.numpy as jnp
from jax import lax
import numpy as np

D_MODEL = 1024
BATCH = 1
SEQ = 256
DEPTH = 2
DEC_BATCH = 8
DEC_SEQ = 1
PAST_LEN = 1024
PAGE_SIZE = 128

N_A_LAYERS = DEPTH // 2
N_B_LAYERS = DEPTH - N_A_LAYERS
CHUNK = 128
D_SGU = 2 * D_MODEL
SGU_GROUPS = 8
SGU_GROUP_DIM = D_SGU // SGU_GROUPS
N_HEADS = 16
QK_NOPE_DIM = 128
QK_ROPE_DIM = 64
V_HEAD_DIM = 128
Q_LORA_RANK = 384
KV_LORA_RANK = 256
ROPE_THETA = 10000.0
D_FF = -(-8 * D_MODEL // (3 * 256)) * 256
ATTN_SCALE = (QK_NOPE_DIM + QK_ROPE_DIM) ** -0.5
EPS = 1e-6
Q_BLOCK = 128

kernel_name = "yoco_chunk_sgu_mla_decoder_step"

def rmsnorm(x, g):
    xf = x.astype(jnp.float32)
    y = xf * lax.rsqrt(jnp.mean(xf * xf, axis=-1, keepdims=True) + EPS)
    return (y * g.astype(jnp.float32)).astype(x.dtype)

def rope(x, pos):
    inv = ROPE_THETA ** (-jnp.arange(0, QK_ROPE_DIM, 2, dtype=jnp.float32) / QK_ROPE_DIM)
    ang = pos[:, None] * inv[None, :]
    ang = ang.reshape((ang.shape[0],) + (1,) * (x.ndim - 3) + (ang.shape[1],))
    cos, sin = jnp.cos(ang), jnp.sin(ang)
    x1, x2 = jnp.split(x.astype(jnp.float32), 2, axis=-1)
    return jnp.concatenate([x1 * cos - x2 * sin, x2 * cos + x1 * sin], axis=-1).astype(x.dtype)

def swiglu(h, w_in, w_out):
    g, u = jnp.split(h @ w_in, 2, axis=-1)
    return (jax.nn.silu(g) * u) @ w_out

def chunk_sgu(h, w_in, v_norm, w_s, b_s, w_out):
    z = jax.nn.gelu(h @ w_in)
    u, v = jnp.split(z, 2, axis=-1)
    v = rmsnorm(v, v_norm)
    B, L, _ = v.shape
    Lp = -(-L // CHUNK) * CHUNK
    vp = jnp.pad(v, ((0, 0), (0, Lp - L), (0, 0)))
    vc = vp.reshape(B, Lp // CHUNK, CHUNK, SGU_GROUPS, SGU_GROUP_DIM)
    ws = w_s * jnp.tril(jnp.ones((CHUNK, CHUNK), dtype=w_s.dtype))
    mixed = jnp.einsum('gts,bcsgd->bctgd', ws, vc) + jnp.transpose(b_s)[:, :, None]
    mixed = mixed.reshape(B, Lp, D_SGU)[:, :L]
    return (u * mixed) @ w_out, v

def shared_kv(h, norm_g, w_dkv, lat_norm, pos):
    ckr = rmsnorm(h, norm_g) @ w_dkv
    c = rmsnorm(ckr[..., :KV_LORA_RANK], lat_norm)
    kr = rope(ckr[..., KV_LORA_RANK:], pos)
    return c, kr

def mla_query(hn, w_dq, q_norm, w_uq, w_uk, pos):
    B, L, _ = hn.shape
    cq = rmsnorm(hn @ w_dq, q_norm)
    q = (cq @ w_uq).reshape(B, L, N_HEADS, QK_NOPE_DIM + QK_ROPE_DIM)
    q_nope, q_rope = q[..., :QK_NOPE_DIM], q[..., QK_NOPE_DIM:]
    q_rope = rope(q_rope, pos)
    q_lat = jnp.einsum('blhd,chd->blhc', q_nope, w_uk)
    return q_lat, q_rope

def attend_prompt(q_lat, q_rope, c, kr):
    B, L = q_lat.shape[:2]
    qb = min(Q_BLOCK, L)
    nb = L // qb
    ql = q_lat.reshape(B, nb, qb, N_HEADS, KV_LORA_RANK).transpose(1, 0, 2, 3, 4)
    qr = q_rope.reshape(B, nb, qb, N_HEADS, QK_ROPE_DIM).transpose(1, 0, 2, 3, 4)
    kpos = jnp.arange(L)

    def block(args):
        i, qlb, qrb = args
        s = (jnp.einsum('bqhc,bkc->bhqk', qlb, c, preferred_element_type=jnp.float32)
             + jnp.einsum('bqhr,bkr->bhqk', qrb, kr, preferred_element_type=jnp.float32)) * ATTN_SCALE
        qpos = i * qb + jnp.arange(qb)
        s = jnp.where(kpos[None, :] <= qpos[:, None], s, -jnp.inf)
        p = jax.nn.softmax(s, axis=-1).astype(c.dtype)
        return jnp.einsum('bhqk,bkc->bqhc', p, c)

    o = lax.map(block, (jnp.arange(nb), ql, qr))
    return o.transpose(1, 0, 2, 3, 4).reshape(B, L, N_HEADS, KV_LORA_RANK)

def attend_sample(q_lat, q_rope, c_new, kr_new, c_past, kr_past):
    s_past = (jnp.einsum('bqhc,bkc->bhqk', q_lat, c_past, preferred_element_type=jnp.float32)
              + jnp.einsum('bqhr,bkr->bhqk', q_rope, kr_past, preferred_element_type=jnp.float32))
    s_new = (jnp.einsum('bqhc,bkc->bhqk', q_lat, c_new, preferred_element_type=jnp.float32)
             + jnp.einsum('bqhr,bkr->bhqk', q_rope, kr_new, preferred_element_type=jnp.float32))
    n = c_new.shape[1]
    s_new = jnp.where(jnp.tril(jnp.ones((n, n), dtype=bool)), s_new, -jnp.inf)
    s = jnp.concatenate([s_past, s_new], axis=-1) * ATTN_SCALE
    p = jax.nn.softmax(s, axis=-1).astype(c_new.dtype)
    P = c_past.shape[1]
    return (jnp.einsum('bhqk,bkc->bqhc', p[..., :P], c_past)
            + jnp.einsum('bhqk,bkc->bqhc', p[..., P:], c_new))

def trunk(x, pos, attend, norm_mix, sgu_w_in, sgu_v_norm, sgu_w_s, sgu_b_s, sgu_w_out,
          norm_ffn, ffn_w_in, ffn_w_out, kv_norm, w_dkv, kv_latent_norm, w_uk, w_uv,
          w_dq, q_norm, w_uq, w_o, final_norm):
    h = x
    v_rows = []
    c = kr = None
    for l in range(DEPTH):
        hn = rmsnorm(h, norm_mix[l])
        if l < N_A_LAYERS:
            a_out, v = chunk_sgu(hn, sgu_w_in[l], sgu_v_norm[l], sgu_w_s[l], sgu_b_s[l], sgu_w_out[l])
            h = h + a_out
            v_rows.append(v)
        else:
            j = l - N_A_LAYERS
            q_lat, q_rope = mla_query(hn, w_dq[j], q_norm[j], w_uq[j], w_uk, pos)
            o_lat = attend(q_lat, q_rope, c, kr)
            o = jnp.einsum('blhc,chv->blhv', o_lat, w_uv)
            h = h + o.reshape(o.shape[0], o.shape[1], N_HEADS * V_HEAD_DIM) @ w_o[j]
        h = h + swiglu(rmsnorm(h, norm_ffn[l]), ffn_w_in[l], ffn_w_out[l])
        if l == N_A_LAYERS - 1:
            c, kr = shared_kv(h, kv_norm, w_dkv, kv_latent_norm, pos)
    return rmsnorm(h, final_norm), c, kr, jnp.stack(v_rows)

def setup_inputs(seed: int = 0) -> dict:
    key = jax.random.key(seed)
    ks = jax.random.split(key, 26)
    f32 = jnp.float32

    def w(k, shape, fan_in):
        return jax.random.normal(k, shape, f32) * fan_in ** -0.5

    def gain(k, shape):
        return 1.0 + 0.05 * jax.random.normal(k, shape, f32)

    n_pages = PAST_LEN // PAGE_SIZE
    n_used = DEC_BATCH * n_pages
    n_phys = n_used + max(1, n_used // 4)
    perm = jax.random.permutation(ks[3], n_phys)[:n_used]
    page_table = perm.reshape(DEC_BATCH, n_pages).astype(jnp.int32)

    return {
        "x_prompt": jax.random.normal(ks[0], (BATCH, SEQ, D_MODEL), f32),
        "x_sample": jax.random.normal(ks[1], (DEC_BATCH, DEC_SEQ, D_MODEL), f32),
        "cache_kv_latent": jax.random.normal(ks[2], (n_phys, PAGE_SIZE, KV_LORA_RANK), f32),
        "cache_k_rope": jax.random.normal(ks[4], (n_phys, PAGE_SIZE, QK_ROPE_DIM), f32),
        "page_table": page_table,
        "norm_mix": gain(ks[5], (DEPTH, D_MODEL)),
        "sgu_w_in": w(ks[6], (N_A_LAYERS, D_MODEL, 2 * D_SGU), D_MODEL),
        "sgu_v_norm": gain(ks[7], (N_A_LAYERS, D_SGU)),
        "sgu_w_s": 0.5 * w(ks[8], (N_A_LAYERS, SGU_GROUPS, CHUNK, CHUNK), CHUNK),
        "sgu_b_s": 1.0 + 0.1 * jax.random.normal(ks[9], (N_A_LAYERS, SGU_GROUPS, CHUNK), f32),
        "sgu_w_out": w(ks[10], (N_A_LAYERS, D_SGU, D_MODEL), D_SGU),
        "norm_ffn": gain(ks[11], (DEPTH, D_MODEL)),
        "ffn_w_in": w(ks[12], (DEPTH, D_MODEL, 2 * D_FF), D_MODEL),
        "ffn_w_out": w(ks[13], (DEPTH, D_FF, D_MODEL), D_FF),
        "kv_norm": gain(ks[14], (D_MODEL,)),
        "w_dkv": w(ks[15], (D_MODEL, KV_LORA_RANK + QK_ROPE_DIM), D_MODEL),
        "kv_latent_norm": gain(ks[16], (KV_LORA_RANK,)),
        "w_uk": w(ks[17], (KV_LORA_RANK, N_HEADS, QK_NOPE_DIM), KV_LORA_RANK),
        "w_uv": w(ks[18], (KV_LORA_RANK, N_HEADS, V_HEAD_DIM), KV_LORA_RANK),
        "w_dq": w(ks[19], (N_B_LAYERS, D_MODEL, Q_LORA_RANK), D_MODEL),
        "q_norm": gain(ks[20], (N_B_LAYERS, Q_LORA_RANK)),
        "w_uq": w(ks[21], (N_B_LAYERS, Q_LORA_RANK, N_HEADS * (QK_NOPE_DIM + QK_ROPE_DIM)), Q_LORA_RANK),
        "w_o": w(ks[22], (N_B_LAYERS, N_HEADS * V_HEAD_DIM, D_MODEL), N_HEADS * V_HEAD_DIM),
        "final_norm": gain(ks[23], (D_MODEL,)),
    }

def reference(x_prompt, x_sample, cache_kv_latent, cache_k_rope, page_table,
              norm_mix, sgu_w_in, sgu_v_norm, sgu_w_s, sgu_b_s, sgu_w_out,
              norm_ffn, ffn_w_in, ffn_w_out, kv_norm, w_dkv, kv_latent_norm, w_uk, w_uv,
              w_dq, q_norm, w_uq, w_o, final_norm):
    params = (norm_mix, sgu_w_in, sgu_v_norm, sgu_w_s, sgu_b_s, sgu_w_out,
              norm_ffn, ffn_w_in, ffn_w_out, kv_norm, w_dkv, kv_latent_norm, w_uk, w_uv,
              w_dq, q_norm, w_uq, w_o, final_norm)

    pos_p = jnp.arange(x_prompt.shape[1], dtype=jnp.float32)
    y_prompt, kv_latent_prompt, k_rope_prompt, _ = trunk(x_prompt, pos_p, attend_prompt, *params)

    n_seq, n_pages = page_table.shape
    c_past = cache_kv_latent[page_table].reshape(n_seq, n_pages * PAGE_SIZE, KV_LORA_RANK)
    kr_past = cache_k_rope[page_table].reshape(n_seq, n_pages * PAGE_SIZE, QK_ROPE_DIM)
    pos_s = jnp.arange(x_sample.shape[1], dtype=jnp.float32) + PAST_LEN
    attend_s = functools.partial(attend_sample, c_past=c_past, kr_past=kr_past)
    y_sample, kv_latent_sample, k_rope_sample, sgu_v_sample = trunk(x_sample, pos_s, attend_s, *params)

    return (y_prompt, y_sample, kv_latent_prompt, k_rope_prompt, kv_latent_sample, k_rope_sample, sgu_v_sample)


_drawn_inputs = setup_inputs


def setup_inputs(seed=0):
    import zlib

    import numpy as np

    out = dict(_drawn_inputs(seed))
    spreads = {}
    factors = {'q_norm': 8.0}
    for name, (base, spread) in spreads.items():
        noise = np.random.default_rng([zlib.crc32(name.encode()), seed]).standard_normal(out[name].shape)
        drawn = base * np.exp(spread * noise) if base else spread * noise
        out[name] = __import__('jax').numpy.asarray(drawn.astype(out[name].dtype))
    for name, factor in factors.items():
        out[name] = (out[name] * factor).astype(out[name].dtype)
    return out
```

```python
from contextlib import ExitStack

import numpy as np
import concourse.bass as bass
from concourse import mybir

F32 = mybir.dt.float32
F32R = mybir.dt.float32r
I32 = mybir.dt.int32
ACT = mybir.ActivationFunctionType
ALU = mybir.AluOpType
AX = mybir.AxisListType.X

P = 128
D = 1024
NP_, NS = 256, 8
T = NP_ + NS
KD = D // P
DS = 2048
KS = DS // P
GROUPS = 8
FF = 2816
KF = FF // P
H = 16
PAIRS = H // 2
LAT, ROPE, NOPE = 256, 64, 128
KL = LAT // P
QR = 384
KQ = QR // P
PAGES, PHYS = 8, 80
KEYT = LAT + ROPE
HALF = PAGES // 2
SCALE = float((NOPE + ROPE) ** -0.5)
EPS = 1e-6
NEG = -3.0e38
PAST = 1024
THETA = 10000.0

BLK = 8
SLAB = BLK * P
RING = 4
AHEAD = 3
BANKS = 4
FO = 3

STAGES = {}
_s = _n = 0
for _name, _chunks, _slabs in (("v", KS, KS), ("u", KS, KS), ("so", KD, 2 * KD), ("fi0", 2 * KF, 2 * KF),
                               ("fo0", KD, FO * KD), ("dq", KQ, KQ), ("kv", 4, 4), ("hd", 8 * PAIRS, 2 * PAIRS),
                               ("wo", KD, 2 * KD), ("fi1", 2 * KF, 2 * KF), ("fo1", KD, FO * KD)):
    STAGES[_name] = (_s, _n)
    _s += _slabs
    _n += _chunks
SLABS = _s

NORMS = [("mix0", D, KD), ("v", DS, KS), ("ffn0", D, KD), ("mix1", D, KD), ("q", QR, KQ), ("lat", LAT, KL),
         ("ffn1", D, KD), ("final", D, KD)]
NQ = {name: q for q, (name, _, _) in enumerate(NORMS)}
ACC0 = [1 + sum(n + 1 for _, _, n in NORMS[:q]) for q in range(len(NORMS))]
SQ0 = [sum(n for _, _, n in NORMS[:q]) for q in range(len(NORMS))]
STEPS = 5


def wait(eng, sem, c, i=0, k=0):
    if isinstance(i, int):
        if c + k * i > 0:
            eng.wait_ge(sem, c + k * i)
    else:
        eng.wait_ge(sem, i * k + c if k else c)


def build(nc, xT, w_stream, w_uv, gains, v_gain, lat_gain, q_gain, wsT, ws00_in, bs, cosT, sinT, keysT, rows, table,
          y_out, c_out, kr_out, v_out):
    with ExitStack() as ctx:
        def sb(name, shape, dt=F32, c=ctx):
            return c.enter_context(nc.sbuf_tensor(name, shape, dt))

        def sem(name):
            return ctx.enter_context(nc.semaphore(name))

        ps = ctx.enter_context(nc.psum_tensor("ps", [P, 8, 512], F32))

        raw = sb("raw", [P, RING, SLAB])
        whi = sb("whi", [P, RING, SLAB], F32R)
        wlo = sb("wlo", [P, RING, SLAB], F32R)
        h = sb("h", [P, KD, T])
        xhi = sb("xhi", [P, KD, T], F32R)
        xlo = sb("xlo", [P, KD, T], F32R)
        ident = sb("ident", [P, P])
        ones = sb("ones", [P, P])
        Ra = sb("Ra", [P, T])
        Rb = sb("Rb", [P, T])
        Rc = sb("Rc", [P, T])
        ms = sb("ms", [P, T])
        yr = sb("yr", [P, T])
        yy = sb("yy", [P, T])
        acc = sb("acc", [P, T])
        sq = sb("sq", [P, 2, T])
        tt = sb("tt", [P, 3, T])
        eps = sb("eps", [P, 1])
        gn = sb("gn", [P, 6, KD, 1])
        gv = sb("gv", [P, KS, 1])
        gl = sb("gl", [P, KL, 1])
        gq = sb("gq", [P, KQ, 1])
        tab = sb("tab", [1, NS * PAGES], I32)
        G = {"mix0": 0, "mix1": 1, "ffn0": 2, "ffn1": 3, "kv": 4, "final": 5}

        cosb = sb("cosb", [P, T])
        sinb = sb("sinb", [P, T])
        mask = sb("mask", [P, 3 * P])
        masks = sb("masks", [H, NS, NS])

        with ExitStack() as a:
            v = sb("v", [P, KS, T], c=a)
            wsraw = sb("wsraw", [P, GROUPS, P], c=a)
            wshi = sb("wshi", [P, GROUPS, P], F32R, a)
            wslo = sb("wslo", [P, GROUPS, P], F32R, a)
            bsb = sb("bsb", [P, GROUPS, P], c=a)
            ws00 = sb("ws00", [P, GROUPS, 1], c=a)
            vn = sb("vn", [P, 2, NP_], c=a)
            vs = sb("vs", [P, KS, NS], c=a)
            vthi = sb("vthi", [P, 2, 2, P], F32R, a)
            vtlo = sb("vtlo", [P, 2, 2, P], F32R, a)
            u = sb("u", [P, 2, T], c=a)
            mb = sb("mb", [P, 2, T], c=a)
            gt = sb("gt", [P, 2, T], c=a)
            ghi = sb("ghi", [P, KS, T], F32R, a)
            glo = sb("glo", [P, KS, T], F32R, a)

        with ExitStack() as f:
            ahi = sb("ahi", [P, KF, T], F32R, f)
            alo = sb("alo", [P, KF, T], F32R, f)
            f_end = sb("f_end", [P, 1], c=f)

        uvhi = sb("uvhi", [P, H * KL, P], F32R)
        uvlo = sb("uvlo", [P, H * KL, P], F32R)
        cT = sb("cT", [P, KL, T])
        kr = sb("kr", [P, T])
        cThi = sb("cThi", [P, KL, NP_], F32R)
        cTlo = sb("cTlo", [P, KL, NP_], F32R)
        cNs = sb("cNs", [NS, LAT])
        with ExitStack() as n:
            cNhi = sb("cNhi", [P, 2, LAT], F32R, n)
            cNlo = sb("cNlo", [P, 2, LAT], F32R, n)
            krzhi = sb("krzhi", [P, 2, NP_], F32R, n)
            krzlo = sb("krzlo", [P, 2, NP_], F32R, n)
        rows0 = sb("rows0", [P, PAGES, LAT])
        mxh = sb("mxh", [P, 2, 2])
        nmh = sb("nmh", [P, 2, 2])
        rsh = sb("rsh", [P, 2, 2])
        rih = sb("rih", [P, 2, 2])
        ohi = sb("ohi", [P, H, T], F32R)
        olo = sb("olo", [P, H, T], F32R)
        x2hi = ohi[:, 0:KD, :]
        x2lo = olo[:, 0:KD, :]
        qsl = sb("qsl", [P, KL, NS, H])
        qsr = sb("qsr", [P, 2, NS, H])
        with ExitStack() as b:
            cqhi = sb("cqhi", [P, KQ, T], F32R, b)
            cqlo = sb("cqlo", [P, KQ, T], F32R, b)
            with ExitStack() as b1:
                uvraw = sb("uvraw", [P, H * KL, P], c=b1)
            with ExitStack() as b2:
                qnhi = sb("qnhi", [P, 2, T], F32R, b2)
                qnlo = sb("qnlo", [P, 2, T], F32R, b2)
                qrhi = sb("qrhi", [P, T], F32R, b2)
                qrlo = sb("qrlo", [P, T], F32R, b2)
                qlhi = sb("qlhi", [P, 2, KL, T], F32R, b2)
                qllo = sb("qllo", [P, 2, KL, T], F32R, b2)
                b2_end = sb("b2_end", [P, 1], c=b2)
                pr = sb("pr", [P, 2, 3 * P], c=b2)
        pthi = xhi[:, 4:7, :].rearrange("p a b -> p (a b)")[:, 0:6 * P].rearrange("p (e k) -> p e k", e=2)
        ptlo = xlo[:, 4:7, :].rearrange("p a b -> p (a b)")[:, 0:6 * P].rearrange("p (e k) -> p e k", e=2)
        olhi = xhi[:, 0:4, :].rearrange("p a b -> p (a b)")[:, 0:8 * P].rearrange("p (e c k) -> p e c k", e=2, c=KL)
        ollo = xlo[:, 0:4, :].rearrange("p a b -> p (a b)")[:, 0:8 * P].rearrange("p (e c k) -> p e c k", e=2, c=KL)

        kt = sb("kt", [P, 2, PAGES, KEYT])
        pr_end = sb("pr_end", [P, 2 * 3 * P + P // 2])
        rows1 = sb("rows1", [P, PAGES, LAT])
        row_of = (rows0, rows1)
        qf = sb("qf", [P, 2, 4, H])
        nm = sb("nm", [H, 2, 1])
        rs = sb("rs", [H, 2, 3])
        rt = sb("rt", [H, 2, 1])
        ri = sb("ri", [H, 2, 1])
        mxs = sb("mxs", [H, 2, 1])
        mxn = sb("mxn", [H, NS, 1])
        nsc = sb("nsc", [H, NS, NS])
        probs = (sq[0:H].rearrange("p a t -> p (a t)")[:, 0:HALF * P],
                 tt[0:H].rearrange("p a t -> p (a t)")[:, 0:HALF * P])
        probs_new = tt[0:H].rearrange("p a t -> p (a t)")[:, HALF * P:HALF * P + NS]
        pT = yr[:, 0:PAGES * H].rearrange("p (g h) -> p g h", g=PAGES)
        pT_new = yr[0:NS, PAGES * H:(PAGES + 1) * H]
        os_ = (ms[0:H, 0:LAT], yy[0:H, 0:LAT])
        ns_row = tt[0:NS, 2, 0:NS * H]
        ols = Rc[:, 0:NS * KL * H].rearrange("p (s x) -> p s x", s=NS)
        olshi = xhi[:, 7:8, 0:KL * H * NS].rearrange("p a (c h s) -> p (a c) h s", c=KL, h=H)
        olslo = xlo[:, 7:8, 0:KL * H * NS].rearrange("p a (c h s) -> p (a c) h s", c=KL, h=H)


        raw_ready = [sem(f"raw_ready{r}") for r in range(RING)]
        h_in, gains_in, sgu_in, rope_in, uv_in, tab_in = map(sem, ("h_in", "gains_in", "sgu_in", "rope_in", "uv_in", "tab_in"))
        keys_ready = [sem(f"keys_ready{r}") for r in range(2)]
        rows_ready = [sem(f"rows_ready{r}") for r in range(2)]
        v_saved, ckr_saved, y_saved = map(sem, ("v_saved", "ckr_saved", "y_saved"))
        const_done, wsm_done = map(sem, ("const_done", "wsm_done"))
        hi_ready, lo_ready, slab_used = map(sem, ("hi_ready", "lo_ready", "slab_used"))
        psum_read = sem("psum_read")
        sq_done, acc_done, sum_done, root_done, norm_step, rms_ready = map(
            sem, ("sq_done", "acc_done", "sum_done", "root_done", "norm_step", "rms_ready"))
        xhi_done, xlo_done = map(sem, ("xhi_done", "xlo_done"))
        gelu_done, wshi_done, wslo_done, vn_done, vs_done, vt_done, vthi_done, vtlo_done = map(
            sem, ("gelu_done", "wshi_done", "wslo_done", "vn_done", "vs_done", "vt_done", "vthi_done", "vtlo_done"))
        mix_done, mixr_done, mbs_done, gt_done, ghi_done, glo_done = map(
            sem, ("mix_done", "mixr_done", "mbs_done", "gt_done", "ghi_done", "glo_done"))
        silu_done, act_done, ahi_done, alo_done = map(sem, ("silu_done", "act_done", "ahi_done", "alo_done"))
        cqhi_done, cqlo_done, rope_step, kr_done, krz_done, krhi_done, krlo_done = map(
            sem, ("cqhi_done", "cqlo_done", "rope_step", "kr_done", "krz_done", "krhi_done", "krlo_done"))
        c_done, cthi_done, ctlo_done, cn_done, cnhi_done, cnlo_done, cns_done, rcs_done, uvhi_done, uvlo_done = map(
            sem, ("c_done", "cthi_done", "ctlo_done", "cn_done", "cnhi_done", "cnlo_done", "cns_done", "rcs_done",
                  "uvhi_done", "uvlo_done"))
        q_done, qnhi_done, qnlo_done, qr_done, qrhi_done, qrlo_done, qlhi_done, qs_done = map(
            sem, ("q_done", "qnhi_done", "qnlo_done", "qr_done", "qrhi_done", "qrlo_done", "qlhi_done", "qs_done"))
        sc_done, sm_done, max_done, nm_done, exp_done, ri_done, pn_done, pt_done, pthi_done, ptlo_done = map(
            sem, ("sc_done", "sm_done", "max_done", "nm_done", "exp_done", "ri_done", "pn_done", "pt_done",
                  "pthi_done", "ptlo_done"))
        pv_done, olhi_done, ollo_done, uv_done, ohi_done, olo_done = map(
            sem, ("pv_done", "olhi_done", "ollo_done", "uv_done", "ohi_done", "olo_done"))
        snT_done, snr_done, snt_done, nsc_done, mxn_done, qsr_done, qf_done = map(
            sem, ("snT_done", "snr_done", "snt_done", "nsc_done", "mxn_done", "qsr_done", "qf_done"))
        ssc_done, mxs_done, snm_done, sexp_done, srt_done, sri_done, spt_done, ptc_done, spv_done, os_done = map(
            sem, ("ssc_done", "mxs_done", "snm_done", "sexp_done", "srt_done", "sri_done", "spt_done", "ptc_done",
                  "spv_done", "os_done"))
        olt_done, ols_done, olshi_done, olslo_done = map(sem, ("olt_done", "ols_done", "olshi_done", "olslo_done"))
        uvs_done, ohis_done, olos_done, y_done = map(sem, ("uvs_done", "ohis_done", "olos_done", "y_done"))

        X0 = {"mix0": 0, "ffn0": KD, "mix1": 2 * KD, "ffn1": 4 * KD}
        HD_S, HD_N = STAGES["hd"]

        def pages_of(e, t, i, out, source, ready):
            for g in range(PAGES):
                at = e.value_load(tab[0:1, bass.ds(i * (2 * PAGES) + (t * PAGES + g), 1)], min_val=0, max_val=PHYS - 1)
                e.dma_start(out[:, g, :], source[at]).then_inc(ready, 16)

        block = ctx.enter_context(nc.Block())

        @block.sync
        def _(sp):
            sp.dma_start(h[:], xT.rearrange("(k p) t -> p k t", p=P)).then_inc(h_in, 16)
            sp.dma_start(gn[:].rearrange("p g k o -> p (g k o)"), gains).then_inc(gains_in, 16)

            def load(c, i=0, k=0):
                wait(sp, lo_ready, c - RING + 1, i, k)
                sp.dma_start(raw[:, c % RING, :], w_stream[i * k + c if k else c]).then_inc(raw_ready[c % RING], 16)

            for c in range(RING):
                load(c)
            sp.dma_start(tab[:], table).then_inc(tab_in, 16)
            first = (STAGES["wo"][0] + AHEAD + RING) // RING
            with sp.Fori(1, first) as i:
                for c in range(RING):
                    load(c, i, RING)
            done = first * RING
            for c in range(done, STAGES["wo"][0] + AHEAD + RING):
                load(c)
            done = STAGES["wo"][0] + AHEAD + RING
            sp.wait_ge(tab_in, 16)
            sp.wait_ge(sc_done, H)

            def load_keys(t, i):
                wait(sp, ssc_done, t - 1, i, 2)
                pages_of(sp, t, i, kt[:, t], keysT, keys_ready[t])

            for t in range(2):
                load_keys(t, 0)
            with sp.Fori(1, NS // 2) as i:
                for t in range(2):
                    load_keys(t, i)
            while done % RING:
                load(done)
                done += 1
            with sp.Fori(0, (SLABS - done) // RING) as i:
                for c in range(RING):
                    load(done + c, i, RING)
            for c in range(done + (SLABS - done) // RING * RING, SLABS):
                load(c)
            for m in range(0, KD, 2):
                sp.wait_ge(y_done, m + 2)
                sp.dma_start(y_out[:, m:m + 2, :], h[:, m:m + 2, :]).then_inc(y_saved, 16)
            sp.wait_ge(y_saved, 16 * KD // 2)

        @block.gpsimd
        def _(pool):
            pool.dma_start(gv[:].rearrange("p k o -> p (k o)"), v_gain).then_inc(sgu_in, 16)
            pool.dma_start(wsraw[:], wsT).then_inc(sgu_in, 16)
            pool.dma_start(bsb[:].rearrange("p g t -> p (g t)"), bs).then_inc(sgu_in, 16)
            pool.dma_start(ws00[:].rearrange("p g o -> p (g o)"), ws00_in).then_inc(sgu_in, 16)
            pool.dma_start(cosb[:], cosT).then_inc(rope_in, 16)
            pool.dma_start(sinb[:], sinT).then_inc(rope_in, 16)
            pool.dma_start(gl[:].rearrange("p k o -> p (k o)"), lat_gain).then_inc(rope_in, 16)
            pool.dma_start(gq[:].rearrange("p k o -> p (k o)"), q_gain).then_inc(rope_in, 16)
            pool.memset(ones[:], 1.0).then_inc(const_done, 1)
            pool.memset(eps[:], EPS).then_inc(const_done, 1)
            pool.memset(ident[:], 0.0).then_inc(const_done, 1)
            pool.memset(mask[:], 0.0).then_inc(const_done, 1)
            pool.memset(masks[:], 0.0).then_inc(const_done, 1)
            pool.wait_ge(const_done, 5)
            pool.affine_select(out=ident[:], in_=ident[:], compare_op=ALU.not_equal, fill=1.0, base=0,
                               pattern=[[-1, P]], channel_multiplier=1).then_inc(const_done, 1)
            for at in (0, 2 * P):
                pool.affine_select(out=mask[:, at:at + P], in_=mask[:, at:at + P], compare_op=ALU.is_ge, fill=NEG,
                                   base=0, pattern=[[-1, P]], channel_multiplier=1).then_inc(const_done, 1)
            for sign in (1, -1):
                pool.affine_select(out=masks[:], in_=masks[:], compare_op=ALU.is_ge, fill=NEG, base=0,
                                   pattern=[[-sign, NS], [sign, NS]], channel_multiplier=0).then_inc(const_done, 1)
                pool.wait_ge(const_done, 9 if sign == 1 else 10)
            pool.wait_ge(sgu_in, 64)
            pool.affine_select(out=wsraw[:], in_=wsraw[:], compare_op=ALU.is_ge, fill=0.0, base=0,
                               pattern=[[0, GROUPS], [1, P]], channel_multiplier=-1).then_inc(wsm_done, 1)
            pool.wait_ge(vs_done, KS)
            pool.dma_start(v_out, vs[:]).then_inc(v_saved, 16)
            wait(pool, slab_used, STAGES["dq"][0])
            pool.dma_start(uvraw[:], w_uv).then_inc(uv_in, 16)
            pool.wait_ge(c_done, KL)
            pool.dma_start(c_out, cT[:]).then_inc(ckr_saved, 16)
            pool.wait_ge(kr_done, 1)
            pool.dma_start(kr_out, kr[0:ROPE, :]).then_inc(ckr_saved, 16)
            pool.wait_ge(tab_in, 16)

            def load_rows(t, i):
                wait(pool, spv_done, t - 1, i, 2)
                pages_of(pool, t, i, row_of[t], rows, rows_ready[t])

            pool.wait_ge(pv_done, H)
            for t in range(2):
                load_rows(t, 0)
            with pool.Fori(1, NS // 2) as i:
                for t in range(2):
                    load_rows(t, i)
            pool.wait_ge(v_saved, 16)
            pool.wait_ge(ckr_saved, 32)

        @block.scalar
        def _(act):
            def split(c, i=0, k=0):
                if isinstance(i, int) and c + k * i >= SLABS:
                    return
                wait(act, raw_ready[c % RING], 16 * (c // RING + 1), i, 16 * k // RING)
                wait(act, slab_used, c - RING + 1, i, k)
                act.activation(whi[:, c % RING, :], raw[:, c % RING, :], ACT.Copy).then_inc(hi_ready, 1)

            def square(q, m, src, i=0, k=0):
                wait(act, acc_done, ACC0[q] + m - 1, i, k)
                act.activation(sq[:, m % 2, :], src, ACT.Square).then_inc(sq_done, 1)

            def root(name):
                q = NQ[name]
                act.wait_ge(sum_done, q + 1)
                wait(act, rms_ready, q)
                act.activation(yr[:], ps[:, 4, 0:T], ACT.Sqrt, bias=eps[:, 0:1],
                               scale=1.0 / NORMS[q][1]).then_inc(root_done, 1)

            def prepare(name, m, i=0, k=0):
                at = i * k + m if k else m
                square(NQ[name], m, h[:, at, :], i, k)
                if name == "final":
                    return
                act.activation(xhi[:, at, :], h[:, at, :], ACT.Copy,
                               scale=gn[:, G[name], at, :]).then_inc(xhi_done, 1)
                if name == "mix1":
                    act.activation(x2hi[:, at, :], h[:, at, :], ACT.Copy,
                                   scale=gn[:, G["kv"], at, :]).then_inc(xhi_done, 1)

            act.wait_ge(h_in, 16)
            act.wait_ge(gains_in, 16)
            for m in range(KD):
                prepare("mix0", m)
            for c in range(AHEAD):
                split(c)
            act.wait_ge(const_done, 10)
            root("mix0")

            def v_chunk(u_, i):
                split(u_ + AHEAD, i, 4)
                wait(act, psum_read, u_ + 1, i, 4)
                act.activation(v[:, i * 4 + u_, :], tt[:, u_ % 2, :], ACT.Gelu_apprx_tanh).then_inc(gelu_done, 1)

            for u_ in range(4):
                v_chunk(u_, 0)
            with act.Fori(1, KS // 4) as i:
                for u_ in range(4):
                    v_chunk(u_, i)
            act.wait_ge(wsm_done, 1)
            act.activation(wshi[:], wsraw[:], ACT.Copy).then_inc(wshi_done, 1)

            def gate_hi(u_, i):
                wait(act, gt_done, u_ + 1, i, 4)
                act.activation(ghi[:, i * 4 + u_, :], gt[:, u_ % 2, :], ACT.Copy).then_inc(ghi_done, 1)

            def u_chunk(u_, i):
                split(KS + u_ + AHEAD, i, 4)
                wait(act, psum_read, KS + u_ + 1, i, 4)
                wait(act, gt_done, u_ - 1, i, 4)
                act.activation(u[:, u_ % 2, :], tt[:, u_ % 2, :], ACT.Gelu_apprx_tanh).then_inc(gelu_done, 1)
                if isinstance(i, int) and u_ == 0:
                    root("v")
                wait(act, vt_done, u_ + 1, i, 4)
                wait(act, mix_done, u_ - 1, i, 4)
                act.activation(vthi[:, u_ % 2, :, :].rearrange("p a b -> p (a b)"), ps[:, 5 + u_ % 2, 0:NP_],
                               ACT.Copy).then_inc(vthi_done, 1)
                if not isinstance(i, int) or u_:
                    gate_hi(u_ - 1, i)

            for u_ in range(4):
                u_chunk(u_, 0)
            with act.Fori(1, KS // 4) as i:
                for u_ in range(4):
                    u_chunk(u_, i)
            gate_hi(KS - 1, 0)

            def residual(stage, name, per, unroll, n):
                s0, n0 = STAGES[stage]

                def chunk(m, i, k):
                    for z in range(per):
                        split(s0 + per * m + AHEAD + z, i, per * k)
                    wait(act, psum_read, n0 + m + 1, i, k)
                    prepare(name, m, i, k)
                if stage == "fo1":
                    for m in range(KD):
                        chunk(m, 0, 0)
                else:
                    with act.Fori(0, KD // unroll) as i:
                        for m in range(unroll):
                            chunk(m, i, unroll)

            def ffn_in(layer):
                s0, n0 = STAGES[f"fi{layer}"]
                A0 = KF * layer

                def pair(w, i):
                    split(s0 + 2 * w + AHEAD, i, 4)
                    wait(act, psum_read, n0 + 2 * w + 1, i, 4)
                    wait(act, alo_done, A0 + w - 1, i, 2)
                    act.activation(sq[:, w % 2, :], tt[:, w % 2, :], ACT.Silu).then_inc(silu_done, 1)
                    split(s0 + 2 * w + AHEAD + 1, i, 4)
                    wait(act, act_done, A0 + w + 1, i, 2)
                    act.activation(ahi[:, i * 2 + w, :], sq[:, w % 2, :], ACT.Copy).then_inc(ahi_done, 1)

                root(f"ffn{layer}")
                if layer == 0:
                    act.wait_ge(v_saved, 16)
                else:
                    act.wait_ge(ckr_saved, 32)
                for w in range(2):
                    pair(w, 0)
                with act.Fori(1, KF // 2) as i:
                    for w in range(2):
                        pair(w, i)

            residual("so", "ffn0", 2, 4, KD)
            ffn_in(0)
            residual("fo0", "mix1", FO, 4, KD)

            s0, n0 = STAGES["dq"]
            root("mix1")
            act.wait_ge(rope_in, 64)
            for d in range(KQ):
                split(s0 + d + AHEAD)
                act.wait_ge(psum_read, n0 + d + 1)
                square(NQ["q"], d, tt[:, d, :])
                act.activation(cqhi[:, d, :], tt[:, d, :], ACT.Copy, scale=gq[:, d, :]).then_inc(cqhi_done, 1)
            s0, n0 = STAGES["kv"]
            for e in range(4):
                split(s0 + e + AHEAD)
                if e == 0:
                    root("q")
                if e < KL:
                    act.wait_ge(psum_read, n0 + e + 1)
                    square(NQ["lat"], e, cT[:, e, :])
            act.wait_ge(kr_done, 1)
            act.wait_ge(krz_done, 4)
            for e in range(2):
                act.activation(krzhi[64 * e:64 * e + 64, e, :], kr[64 * e:64 * e + 64, 0:NP_],
                               ACT.Copy).then_inc(krhi_done, 1)
            root("lat")
            act.wait_ge(c_done, KL)
            act.activation(cThi[:], cT[:, :, 0:NP_], ACT.Copy).then_inc(cthi_done, 1)

            def pair(p, i=0, k=0, q=True, back=True):
                hd = lambda e: 2 * p + e
                n = HD_N + 8 * p
                if back:
                    for e in range(2):
                        wait(act, nm_done, hd(e) - 1, i, 2 * k)
                        for part, (lo, hi_) in enumerate(((0, P), (P, 3 * P))):
                            act.activation(pr[:, e, lo:hi_], pr[:, e, lo:hi_], ACT.Exp, bias=nmh[:, e, part:part + 1],
                                           accum_out=rsh[:, e, part:part + 1]).then_inc(exp_done, 1)
                if q:
                    split(HD_S + 2 * p + AHEAD, i, 2 * k)
                    for e in range(2):
                        wait(act, psum_read, n + e + 1, i, 8 * k)
                        act.activation(qnhi[:, e, :], tt[:, e, :], ACT.Copy).then_inc(qnhi_done, 1)
                    wait(act, qr_done, p + 1, i, k)
                    act.activation(qrhi[:], sq[:, 1, :], ACT.Copy).then_inc(qrhi_done, 1)
                if back:
                    for e in range(2):
                        wait(act, pt_done, hd(e) - 1, i, 2 * k)
                        act.activation(pthi[:, e, :], ps[:, 6 + e, 0:3 * P], ACT.Copy).then_inc(pthi_done, 1)
                if q:
                    for e in range(2):
                        for c in range(KL):
                            if c:
                                wait(act, slab_used, HD_S + 2 * p + e + 1, i, 2 * k)
                            else:
                                wait(act, q_done, 6 * p + 5 + e, i, 6 * k)
                            act.activation(qlhi[:, e, c, :], ps[:, (n + 4 + 2 * e + c) % BANKS, 0:T],
                                           ACT.Copy).then_inc(qlhi_done, 1)
                if back:
                    for e in range(2):
                        wait(act, pv_done, hd(e) - 1, i, 2 * k)
                        act.activation(olhi[:, e].rearrange("p c k -> p (c k)"), ps[:, 6 + e, :],
                                       ACT.Copy).then_inc(olhi_done, 1)
                if q:
                    split(HD_S + 2 * p + AHEAD + 1, i, 2 * k)
                if back:
                    for e in range(2):
                        wait(act, uv_done, hd(e) - 1, i, 2 * k)
                        act.activation(ohi[:, i * (2 * k) + (hd(e) - 2) if k else hd(e) - 2, 0:NP_], ps[:, 6 + e, 0:NP_],
                                       ACT.Copy).then_inc(ohi_done, 1)

            act.wait_ge(cn_done, 2)
            act.activation(cNhi[:].rearrange("p a b -> p (a b)"), ps[:, 6, :], ACT.Copy).then_inc(cnhi_done, 1)
            act.wait_ge(uv_in, 16)
            act.activation(uvhi[:], uvraw[:], ACT.Copy).then_inc(uvhi_done, 1)
            pair(0, back=False)
            pair(1)
            with act.Fori(0, PAIRS // 2 - 1) as i:
                for p in (2, 3):
                    pair(p, i, 2)
            pair(PAIRS, q=False)

            def exponentials(t, i):
                wait(act, snm_done, t + 1, i, 2)
                wait(act, spt_done, t, i, 2)
                for half in range(2):
                    act.activation(probs[half], ps[0:H, 2 * t + half, :], ACT.Exp, bias=nm[:, t, :], scale=SCALE,
                                   accum_out=rs[:, t, half:half + 1]).then_inc(sexp_done, 1)
                act.activation(probs_new, nsc[:, i * 2 + t, :], ACT.Exp, bias=nm[:, t, :], scale=SCALE,
                               accum_out=rs[:, t, 2:3]).then_inc(sexp_done, 1)

            def take_out(t, i):
                o = t % 2
                wait(act, olt_done, t + 1, i, 2)
                act.activation(ols[:, i * 2 + t, :], ps[:, 7 - 3 * o, 0:KL * H],
                               ACT.Copy).then_inc(ols_done, 1)

            for t in range(2):
                exponentials(t, 0)
            with act.Fori(1, NS // 2) as i:
                for t in range(2):
                    exponentials(t, i)
                    take_out(t - 2, i)
            take_out(NS - 2, 0)
            take_out(NS - 1, 0)
            act.wait_ge(ols_done, NS)
            act.activation(olshi, ols.rearrange("p s (c h) -> p c h s", c=KL), ACT.Copy).then_inc(olshi_done, 1)
            act.wait_ge(uvs_done, 1)
            act.activation(ohi[:, :, NP_:T], ps[:, 0, 0:H * NS].rearrange("p (a b) -> p a b", a=H),
                           ACT.Copy).then_inc(ohis_done, 1)

            residual("wo", "ffn1", 2, 4, KD)
            ffn_in(1)
            residual("fo1", "final", FO, 4, KD)
            root("final")

        @block.vector
        def _(dve):
            def lo_of(out, full, hi):
                return dve.tensor_tensor(out, full, hi.bitcast(F32), ALU.subtract)

            def split(c, i=0, k=0):
                if isinstance(i, int) and c + k * i >= SLABS:
                    return
                wait(dve, hi_ready, c + 1, i, k)
                lo_of(wlo[:, c % RING, :], raw[:, c % RING, :], whi[:, c % RING, :]).then_inc(lo_ready, 1)

            def add_square(q, m, i=0, k=0):
                wait(dve, sq_done, SQ0[q] + m + 1, i, k)
                wait(dve, acc_done, ACC0[q] + m, i, k)
                dve.tensor_tensor(acc[:], acc[:], sq[:, m % 2, :], ALU.add).then_inc(acc_done, 1)

            def inverse_root(name, R):
                q = NQ[name]
                dve.wait_ge(root_done, q + 1)
                dve.tensor_scalar(ms[:], ps[:, 4, 0:T], 1.0 / NORMS[q][1], EPS, ALU.mult, ALU.add).then_inc(norm_step, 1)
                dve.reciprocal(yr[:], yr[:]).then_inc(norm_step, 1)
                dve.memset(acc[:], 0.0).then_inc(acc_done, 1)
                dve.wait_ge(norm_step, STEPS * q + 2)
                dve.tensor_tensor(yy[:], yr[:], yr[:], ALU.mult).then_inc(norm_step, 1)
                dve.wait_ge(norm_step, STEPS * q + 3)
                dve.tensor_tensor(yy[:], yy[:], ms[:], ALU.mult).then_inc(norm_step, 1)
                dve.wait_ge(norm_step, STEPS * q + 4)
                dve.tensor_scalar(yy[:], yy[:], -0.5, 1.5, ALU.mult, ALU.add).then_inc(norm_step, 1)
                dve.wait_ge(norm_step, STEPS * q + 5)
                dve.tensor_tensor(R[:], yr[:], yy[:], ALU.mult).then_inc(rms_ready, 1)
                dve.wait_ge(rms_ready, q + 1)

            def scaled(out, n, R, i=0, k=0, src=None):
                return dve.tensor_tensor(out, ps[:, n % BANKS, 0:T], R[:], ALU.mult).then_inc(psum_read, 1)

            def prepare(name, m, i=0, k=0):
                at = i * k + m if k else m
                add_square(NQ[name], m, i, k)
                if name == "final":
                    return
                per = 2 if name == "mix1" else 1
                for z, (gain, hi, lo) in enumerate(((name, xhi, xlo), ("kv", x2hi, x2lo))[:per]):
                    wait(dve, xhi_done, X0[name] + per * m + z + 1, i, per * k)
                    dve.scalar_tensor_tensor(out=lo[:, at, :], in0=h[:, at, :], scalar=gn[:, G[gain], at, :],
                                             in1=hi[:, at, :].bitcast(F32), op0=ALU.mult,
                                             op1=ALU.subtract).then_inc(xlo_done, 1)

            dve.memset(acc[:], 0.0).then_inc(acc_done, 1)
            dve.wait_ge(h_in, 16)
            dve.wait_ge(gains_in, 16)
            for m in range(KD):
                prepare("mix0", m)
            for c in range(AHEAD):
                split(c)
            inverse_root("mix0", Ra)

            def v_chunk(u_, i):
                wait(dve, slab_used, u_ + 1, i, 4)
                wait(dve, gelu_done, u_ - 1, i, 4)
                scaled(tt[:, u_ % 2, :], u_, Ra)
                split(u_ + AHEAD, i, 4)
                wait(dve, gelu_done, u_ + 1, i, 4)
                dve.tensor_tensor(sq[:, u_ % 2, :], v[:, i * 4 + u_, :], v[:, i * 4 + u_, :],
                                  ALU.mult).then_inc(sq_done, 1)
                add_square(NQ["v"], u_, i, 4)

            for u_ in range(4):
                v_chunk(u_, 0)
            with dve.Fori(1, KS // 4) as i:
                for u_ in range(4):
                    v_chunk(u_, i)
            dve.wait_ge(wshi_done, 1)
            lo_of(wslo[:], wsraw[:], wshi[:]).then_inc(wslo_done, 1)
            dve.wait_ge(sgu_in, 64)

            def norm_v(u_, i):
                at = i * 4 + u_
                wait(dve, vt_done, u_ - 1, i, 4)
                dve.scalar_tensor_tensor(out=vn[:, u_ % 2, :], in0=v[:, at, 0:NP_], scalar=gv[:, at, :],
                                         in1=Rb[:, 0:NP_], op0=ALU.mult, op1=ALU.mult).then_inc(vn_done, 1)
                dve.scalar_tensor_tensor(out=vs[:, at, :], in0=v[:, at, NP_:T], scalar=gv[:, at, :],
                                         in1=Rb[:, NP_:T], op0=ALU.mult, op1=ALU.mult).then_inc(vs_done, 1)

            def gate(u_, i):
                at = i * 4 + u_
                g = (i * 2 + (u_ // 2))
                slot = u_ % 2
                wait(dve, mix_done, u_ + 1, i, 4)
                dve.tensor_tensor(mb[:, slot, 0:NP_].rearrange("p (a t) -> p a t", a=2),
                                  ps[:, 7, 0:NP_].rearrange("p (a t) -> p a t", a=2),
                                  bsb[:, g, :].unsqueeze(1).broadcast_to([P, 2, P]), ALU.add).then_inc(mixr_done, 1)
                wait(dve, vs_done, u_ + 1, i, 4)
                dve.tensor_scalar(mb[:, slot, NP_:T], vs[:, at, :], ws00[:, g, :], bsb[:, g, 0:1],
                                  ALU.mult, ALU.add).then_inc(mbs_done, 1)
                wait(dve, mixr_done, u_ + 1, i, 4)
                wait(dve, mbs_done, u_ + 1, i, 4)
                wait(dve, gelu_done, KS + u_ + 1, i, 4)
                wait(dve, ghi_done, u_ - 1, i, 4)
                dve.tensor_tensor(gt[:, slot, :], mb[:, slot, :], u[:, slot, :], ALU.mult).then_inc(gt_done, 1)
                wait(dve, ghi_done, u_ + 1, i, 4)
                lo_of(glo[:, at, :], gt[:, slot, :], ghi[:, at, :]).then_inc(glo_done, 1)

            def u_chunk(u_, i):
                first = isinstance(i, int) and u_ == 0
                if not first:
                    norm_v(u_, i)
                wait(dve, slab_used, KS + u_ + 1, i, 4)
                wait(dve, gelu_done, KS + u_ - 1, i, 4)
                scaled(tt[:, u_ % 2, :], u_, Ra)
                split(KS + u_ + AHEAD, i, 4)
                if first:
                    inverse_root("v", Rb)
                    norm_v(u_, i)
                wait(dve, vthi_done, u_ + 1, i, 4)
                wait(dve, mix_done, u_ - 1, i, 4)
                lo_of(vtlo[:, u_ % 2, :, :].rearrange("p a b -> p (a b)"), ps[:, 5 + u_ % 2, 0:NP_],
                      vthi[:, u_ % 2, :, :].rearrange("p a b -> p (a b)")).then_inc(vtlo_done, 1)
                if not first:
                    gate(u_ - 1, i)

            for u_ in range(4):
                u_chunk(u_, 0)
            with dve.Fori(1, KS // 4) as i:
                for u_ in range(4):
                    u_chunk(u_, i)
            gate(KS - 1, 0)

            def residual(stage, name, per, unroll):
                s0, n0 = STAGES[stage]

                def chunk(m, i, k):
                    at = i * k + m if k else m
                    wait(dve, slab_used, s0 + per * (m + 1), i, per * k)
                    dve.tensor_tensor(h[:, at, :], ps[:, (n0 + m) % BANKS, 0:T], h[:, at, :],
                                      ALU.add).then_inc(psum_read, 1)
                    for z in range(per):
                        split(s0 + per * m + AHEAD + z, i, per * k)
                    prepare(name, m, i, k)
                if stage == "fo1":
                    for m in range(KD):
                        chunk(m, 0, 0)
                else:
                    with dve.Fori(0, KD // unroll) as i:
                        for m in range(unroll):
                            chunk(m, i, unroll)

            def ffn_in(layer):
                s0, n0 = STAGES[f"fi{layer}"]
                A0 = KF * layer

                def pair(w, i):
                    wait(dve, slab_used, s0 + 2 * w + 1, i, 4)
                    wait(dve, silu_done, A0 + w - 1, i, 2)
                    scaled(tt[:, w % 2, :], n0 + 2 * w, Ra)
                    split(s0 + 2 * w + AHEAD, i, 4)
                    wait(dve, slab_used, s0 + 2 * w + 2, i, 4)
                    scaled(tt[:, 2, :], n0 + 2 * w + 1, Ra)
                    wait(dve, psum_read, n0 + 2 * w + 2, i, 4)
                    wait(dve, silu_done, A0 + w + 1, i, 2)
                    dve.tensor_tensor(sq[:, w % 2, :], sq[:, w % 2, :], tt[:, 2, :], ALU.mult).then_inc(act_done, 1)
                    split(s0 + 2 * w + AHEAD + 1, i, 4)
                    wait(dve, ahi_done, A0 + w + 1, i, 2)
                    lo_of(alo[:, i * 2 + w, :], sq[:, w % 2, :], ahi[:, i * 2 + w, :]).then_inc(alo_done, 1)

                inverse_root(f"ffn{layer}", Ra)
                if layer == 0:
                    dve.wait_ge(v_saved, 16)
                else:
                    dve.wait_ge(ckr_saved, 32)
                for w in range(2):
                    pair(w, 0)
                with dve.Fori(1, KF // 2) as i:
                    for w in range(2):
                        pair(w, i)

            residual("so", "ffn0", 2, 4)
            ffn_in(0)
            residual("fo0", "mix1", FO, 4)

            s0, n0 = STAGES["dq"]
            inverse_root("mix1", Ra)
            dve.wait_ge(rope_in, 64)
            for d in range(KQ):
                dve.wait_ge(slab_used, s0 + d + 1)
                scaled(tt[:, d, :], n0 + d, Ra)
                split(s0 + d + AHEAD)
                add_square(NQ["q"], d)
                dve.wait_ge(cqhi_done, d + 1)
                dve.scalar_tensor_tensor(out=cqlo[:, d, :], in0=tt[:, d, :], scalar=gq[:, d, :],
                                         in1=cqhi[:, d, :].bitcast(F32), op0=ALU.mult,
                                         op1=ALU.subtract).then_inc(cqlo_done, 1)
            s0, n0 = STAGES["kv"]
            for e in range(2):
                other = slice(64 * (1 - e), 64 * (1 - e) + 64)
                dve.memset(krzhi[other, e, :].bitcast(F32), 0.0).then_inc(krz_done, 1)
                dve.memset(krzlo[other, e, :].bitcast(F32), 0.0).then_inc(krz_done, 1)
            dve.memset(qsr[ROPE:P, 0], 0.0).then_inc(qs_done, 1)
            for e in range(4):
                dve.wait_ge(slab_used, s0 + e + 1)
                if e < KL:
                    scaled(cT[:, e, :], n0 + e, Ra)
                    split(s0 + e + AHEAD)
                    if e == 0:
                        inverse_root("q", Rb)
                    add_square(NQ["lat"], e)
                else:
                    scaled(tt[:, e - KL, :], n0 + e, Ra)
                    split(s0 + e + AHEAD)
            dve.wait_ge(psum_read, n0 + 4)
            dve.tensor_tensor(tt[:, 0, :], tt[:, 0, :], cosb[:], ALU.mult).then_inc(rope_step, 1)
            dve.tensor_tensor(tt[:, 1, :], tt[:, 1, :], sinb[:], ALU.mult).then_inc(rope_step, 1)
            dve.wait_ge(rope_step, 2)
            dve.tensor_tensor(kr[:], tt[:, 0, :], tt[:, 1, :], ALU.add).then_inc(kr_done, 1)
            for e in range(2):
                dve.wait_ge(krhi_done, e + 1)
                lo_of(krzlo[64 * e:64 * e + 64, e, :], kr[64 * e:64 * e + 64, 0:NP_],
                      krzhi[64 * e:64 * e + 64, e, :]).then_inc(krlo_done, 1)
            inverse_root("lat", Rc)
            for c in range(KL):
                dve.scalar_tensor_tensor(out=cT[:, c, :], in0=cT[:, c, :], scalar=gl[:, c, :], in1=Rc[:],
                                         op0=ALU.mult, op1=ALU.mult).then_inc(c_done, 1)
            dve.tensor_tensor(ms[:], Rb[:], cosb[:], ALU.mult).then_inc(rcs_done, 1)
            dve.tensor_tensor(yy[:], Rb[:], sinb[:], ALU.mult).then_inc(rcs_done, 1)
            dve.wait_ge(cthi_done, 1)
            lo_of(cTlo[:], cT[:, :, 0:NP_], cThi[:]).then_inc(ctlo_done, 1)
            dve.wait_ge(cnhi_done, 1)
            lo_of(cNlo[:].rearrange("p a b -> p (a b)"), ps[:, 6, :],
                  cNhi[:].rearrange("p a b -> p (a b)")).then_inc(cnlo_done, 1)
            dve.tensor_copy(cNs[:], ps[0:NS, 7, 0:LAT]).then_inc(cns_done, 1)
            dve.wait_ge(uvhi_done, 1)
            lo_of(uvlo[:], uvraw[:], uvhi[:]).then_inc(uvlo_done, 1)
            dve.wait_ge(uvlo_done, 1)
            dve.wait_ge(rcs_done, 2)

            def pair(p, i=0, k=0, q=True, back=True):
                hd = lambda e: 2 * p + e
                n = HD_N + 8 * p
                if back:
                    for e in range(2):
                        wait(dve, sc_done, hd(e) - 1, i, 2 * k)
                        dve.scalar_tensor_tensor(out=pr[:, e, :], in0=ps[:, 4 + e, 0:3 * P], scalar=SCALE, in1=mask[:],
                                                 op0=ALU.mult, op1=ALU.add).then_inc(sm_done, 1)
                        wait(dve, sm_done, hd(e) - 1, i, 2 * k)
                        dve.tensor_reduce(mxh[:, e, 0:1], pr[:, e, 0:P], AX, ALU.max).then_inc(max_done, 1)
                        dve.tensor_reduce(mxh[:, e, 1:2], pr[:, e, P:3 * P], AX, ALU.max).then_inc(max_done, 1)
                        wait(dve, max_done, 2 * hd(e) - 2, i, 4 * k)
                        dve.tensor_scalar(nmh[:, e, :], mxh[:, e, :], -1.0, None, ALU.mult).then_inc(nm_done, 1)
                    for e in range(2):
                        wait(dve, exp_done, 2 * hd(e) - 2, i, 4 * k)
                        dve.reciprocal(rih[:, e, :], rsh[:, e, :]).then_inc(ri_done, 1)
                        wait(dve, ri_done, hd(e) - 1, i, 2 * k)
                        dve.tensor_scalar(pr[:, e, 0:P], pr[:, e, 0:P], rih[:, e, 0:1], None,
                                          ALU.mult).then_inc(pn_done, 1)
                        dve.tensor_scalar(pr[:, e, P:3 * P], pr[:, e, P:3 * P], rih[:, e, 1:2], None,
                                          ALU.mult).then_inc(pn_done, 1)
                if q:
                    split(HD_S + 2 * p + AHEAD, i, 2 * k)
                    for e in range(2):
                        wait(dve, q_done, 6 * p + e + 1, i, 6 * k)
                        scaled(tt[:, e, :], n + e, Rb)
                    for e in range(2):
                        wait(dve, qnhi_done, hd(e) + 1, i, 2 * k)
                        lo_of(qnlo[:, e, :], tt[:, e, :], qnhi[:, e, :]).then_inc(qnlo_done, 1)
                    wait(dve, q_done, 6 * p + 3, i, 6 * k)
                    scaled(tt[:, 2, :], n + 2, ms)
                    wait(dve, q_done, 6 * p + 4, i, 6 * k)
                    scaled(sq[:, 0, :], n + 3, yy)
                    wait(dve, psum_read, n + 4, i, 8 * k)
                    dve.tensor_tensor(sq[:, 1, :], tt[:, 2, :], sq[:, 0, :], ALU.add).then_inc(qr_done, 1)
                    wait(dve, qrhi_done, p + 1, i, k)
                    lo_of(qrlo[:], sq[:, 1, :], qrhi[:]).then_inc(qrlo_done, 1)
                    for e in range(2):
                        dve.tensor_copy(qsr[0:ROPE, 0, :, i * (2 * k) + hd(e) if k else hd(e)],
                                        sq[64 * e:64 * e + 64, 1, NP_:T]).then_inc(qs_done, 1)
                if back:
                    for e in range(2):
                        wait(dve, pthi_done, hd(e) - 1, i, 2 * k)
                        lo_of(ptlo[:, e, :], ps[:, 6 + e, 0:3 * P], pthi[:, e, :]).then_inc(ptlo_done, 1)
                if q:
                    for e in range(2):
                        for c in range(KL):
                            bank = (n + 4 + 2 * e + c) % BANKS
                            wait(dve, qlhi_done, 4 * p + 2 * e + c + 1, i, 4 * k)
                            dve.tensor_copy(qsl[:, c, :, i * (2 * k) + hd(e) if k else hd(e)],
                                            ps[:, bank, NP_:T]).then_inc(qs_done, 1)
                            lo_of(qllo[:, e, c, :], ps[:, bank, 0:T], qlhi[:, e, c, :]).then_inc(psum_read, 1)
                if back:
                    for e in range(2):
                        wait(dve, olhi_done, hd(e) - 1, i, 2 * k)
                        lo_of(ollo[:, e].rearrange("p c k -> p (c k)"), ps[:, 6 + e, :],
                              olhi[:, e].rearrange("p c k -> p (c k)")).then_inc(ollo_done, 1)
                if q:
                    split(HD_S + 2 * p + AHEAD + 1, i, 2 * k)
                if back:
                    for e in range(2):
                        wait(dve, ohi_done, hd(e) - 1, i, 2 * k)
                        at = i * (2 * k) + (hd(e) - 2) if k else hd(e) - 2
                        lo_of(olo[:, at, 0:NP_], ps[:, 6 + e, 0:NP_], ohi[:, at, 0:NP_]).then_inc(olo_done, 1)

            pair(0, back=False)
            pair(1)
            with dve.Fori(0, PAIRS // 2 - 1) as i:
                for p in (2, 3):
                    pair(p, i, 2)
            pair(PAIRS, q=False)

            dve.wait_ge(qs_done, 6 * PAIRS + 1)
            dve.memset(qsr[0:ROPE, 1], 0.0).then_inc(qsr_done, 1)
            dve.tensor_copy(qsr[ROPE:P, 1], qsr[0:ROPE, 0]).then_inc(qsr_done, 1)
            dve.wait_ge(snT_done, 1)
            dve.tensor_copy(ns_row, ps[0:NS, 4, 0:NS * H]).then_inc(snr_done, 1)
            dve.wait_ge(snt_done, 1)
            dve.tensor_tensor(nsc[:].rearrange("p a b -> p (a b)"), ps[0:H, 5, 0:NS * NS],
                              masks[:].rearrange("p a b -> p (a b)"), ALU.add).then_inc(nsc_done, 1)
            dve.wait_ge(nsc_done, 1)
            dve.tensor_reduce(mxn[:].rearrange("p a b -> p (a b)"), nsc[:], AX, ALU.max).then_inc(mxn_done, 1)
            dve.wait_ge(mxn_done, 1)
            dve.wait_ge(qsr_done, 2)

            def queries_of(t, i):
                wait(dve, ssc_done, t - 1, i, 2)
                at = i * 2 + t
                dve.tensor_copy(qf[:, t, 0:KL, :], qsl[:, :, at, :]).then_inc(qf_done, 1)
                dve.tensor_copy(qf[:, t, KL:4, :], qsr[:, :, at, :]).then_inc(qf_done, 1)

            def maximum(t, i):
                o = t % 2
                wait(dve, ssc_done, t + 1, i, 2)
                dve.tensor_reduce(mxs[:, o, :], ps[0:H, 2 * o:2 * o + 2, :].rearrange("p b k -> p (b k)"), AX,
                                  ALU.max).then_inc(mxs_done, 1)
                wait(dve, mxs_done, t + 1, i, 2)
                dve.tensor_scalar(nm[:, o, :], mxs[:, o, :], mxn[:, i * 2 + t, :], -SCALE, ALU.max, ALU.mult).then_inc(snm_done, 1)

            def rest(t, i):
                o = t % 2
                wait(dve, spt_done, t + 1, i, 2)
                wait(dve, spv_done, t, i, 2)
                dve.tensor_copy(pT, ps[:, 5, 0:PAGES * H].rearrange("p (g h) -> p g h", g=PAGES)).then_inc(ptc_done, 1)
                dve.tensor_copy(pT_new, ps[0:NS, 5, PAGES * H:(PAGES + 1) * H]).then_inc(ptc_done, 1)
                dve.tensor_reduce(rt[:, o, :], rs[:, o, :], AX, ALU.add).then_inc(srt_done, 1)
                wait(dve, srt_done, t + 1, i, 2)
                dve.reciprocal(ri[:, o, :], rt[:, o, :]).then_inc(sri_done, 1)
                wait(dve, sri_done, t + 1, i, 2)
                wait(dve, spv_done, t + 1, i, 2)
                dve.tensor_scalar(os_[o], ps[0:H, 6, o * LAT:(o + 1) * LAT], ri[:, o, :], None,
                                  ALU.mult).then_inc(os_done, 1)

            queries_of(0, 0)
            queries_of(1, 0)
            maximum(0, 0)
            with dve.Fori(1, NS // 2) as i:
                queries_of(0, i)
                maximum(-1, i)
                rest(-2, i)
                queries_of(1, i)
                maximum(0, i)
                rest(-1, i)
            maximum(NS - 1, 0)
            rest(NS - 2, 0)
            rest(NS - 1, 0)
            dve.wait_ge(olshi_done, 1)
            lo_of(olslo, ols.rearrange("p s (c h) -> p c h s", c=KL), olshi).then_inc(olslo_done, 1)
            dve.wait_ge(ohis_done, 1)
            lo_of(olo[:, :, NP_:T], ps[:, 0, 0:H * NS].rearrange("p (a b) -> p a b", a=H),
                  ohi[:, :, NP_:T]).then_inc(olos_done, 1)

            residual("wo", "ffn1", 2, 4)
            ffn_in(1)
            residual("fo1", "final", FO, 4)
            inverse_root("final", Ra)
            for m in range(KD):
                dve.scalar_tensor_tensor(out=h[:, m, :], in0=h[:, m, :], scalar=gn[:, G["final"], m, :], in1=Ra[:],
                                         op0=ALU.mult, op1=ALU.mult).then_inc(y_done, 1)

        @block.tensor
        def _(pe):
            def passes(out, whi_, wlo_, mhi, mlo, start, stop):
                pe.matmul(out, whi_, mhi, start=start, stop=False)
                pe.matmul(out, whi_, mlo, start=False, stop=False)
                return pe.matmul(out, wlo_, mhi, start=False, stop=stop)

            def main(c, n, blocks, rhs, i=0, ks=0, kn=0, ready=None):
                wait(pe, psum_read, n - BANKS + 1, i, kn)
                out = ps[:, n % BANKS, 0:T]
                for b in range(blocks):
                    s, j = c + b // BLK, b % BLK
                    if j == 0:
                        wait(pe, lo_ready, s + 1, i, ks)
                    if ready:
                        ready(b)
                    w = slice(j * P, j * P + P)
                    last = passes(out, whi[:, s % RING, w], wlo[:, s % RING, w], *rhs(b), b == 0, b == blocks - 1)
                    if j == BLK - 1 or b == blocks - 1:
                        last.then_inc(slab_used, 1)

            def norm_sum(name):
                q = NQ[name]
                wait(pe, rms_ready, q)
                pe.wait_ge(acc_done, ACC0[q] + NORMS[q][2])
                pe.matmul(ps[:, 4, 0:T], ones[:], acc[:], start=True, stop=True).then_inc(sum_done, 1)

            x_of = lambda b: (xhi[:, b, :], xlo[:, b, :])

            def x_ready(name, per=1, off=0):
                return lambda b: pe.wait_ge(xlo_done, X0[name] + per * b + off + 1)

            pe.wait_ge(const_done, 10)
            norm_sum("mix0")
            main(0, 0, KD, x_of, ready=x_ready("mix0"))
            for u_ in range(1, 4):
                main(u_, u_, KD, x_of)
            with pe.Fori(1, KS // 4) as i:
                for u_ in range(4):
                    main(u_, u_, KD, x_of, i, 4, 4)

            def mix(u_, i):
                slot = u_ % 2
                wait(pe, vtlo_done, u_ + 1, i, 4)
                wait(pe, mixr_done, u_, i, 4)
                g = i * 2 + u_ // 2
                for a in range(2):
                    last = passes(ps[:, 7, a * P:a * P + P], vthi[:, slot, a, :], vtlo[:, slot, a, :],
                                  wshi[:, g, :], wslo[:, g, :], True, True)
                last.then_inc(mix_done, 1)

            def u_chunk(u_, i):
                first = isinstance(i, int) and u_ == 0
                main(KS + u_, KS + u_, KD, x_of, i, 4, 4)
                if first:
                    norm_sum("v")
                    pe.wait_ge(wslo_done, 1)
                wait(pe, vn_done, u_ + 1, i, 4)
                wait(pe, vtlo_done, u_ - 1, i, 4)
                for a in range(2):
                    last = pe.transpose(ps[:, 5 + u_ % 2, a * P:a * P + P], vn[:, u_ % 2, a * P:a * P + P], ident[:])
                last.then_inc(vt_done, 1)
                if not first:
                    mix(u_ - 1, i)

            for u_ in range(4):
                u_chunk(u_, 0)
            with pe.Fori(1, KS // 4) as i:
                for u_ in range(4):
                    u_chunk(u_, i)
            mix(KS - 1, 0)

            def out_product(stage, per, blocks, rhs, ready):
                s0, n0 = STAGES[stage]
                with pe.Fori(0, KD // 4) as i:
                    for m in range(4):
                        main(s0 + per * m, n0 + m, blocks, rhs, i, 4 * per, 4, ready if m == 0 else None)

            def ffn(layer):
                s0, n0 = STAGES[f"fi{layer}"]
                name = f"ffn{layer}"
                for c in range(4):
                    main(s0 + c, n0 + c, KD, x_of, ready=x_ready(name) if c == 0 else None)
                    if c == 0:
                        norm_sum(name)
                with pe.Fori(1, KF // 2) as i:
                    for c in range(4):
                        main(s0 + c, n0 + c, KD, x_of, i, 4, 4)
                out_product(f"fo{layer}", FO, KF, lambda b: (ahi[:, b, :], alo[:, b, :]),
                            lambda b: pe.wait_ge(alo_done, KF * layer + b + 1))

            out_product("so", 2, KS, lambda b: (ghi[:, b, :], glo[:, b, :]), lambda b: pe.wait_ge(glo_done, b + 1))
            ffn(0)

            s0, n0 = STAGES["dq"]
            for d in range(KQ):
                main(s0 + d, n0 + d, KD, x_of, ready=x_ready("mix1", 2) if d == 0 else None)
                if d == 0:
                    norm_sum("mix1")
            s0, n0 = STAGES["kv"]
            for e in range(4):
                main(s0 + e, n0 + e, KD, lambda b: (x2hi[:, b, :], x2lo[:, b, :]),
                     ready=x_ready("mix1", 2, 1) if e == 0 else None)
                if e == 0:
                    norm_sum("q")
            norm_sum("lat")

            def blocks3(bank, slab, j0):
                w = [slice((j0 + b) * P, (j0 + b + 1) * P) for b in range(KQ)]
                for b in range(KQ):
                    last = passes(ps[:, bank, 0:T], whi[:, slab % RING, w[b]], wlo[:, slab % RING, w[b]],
                                  cqhi[:, b, :], cqlo[:, b, :], b == 0, b == KQ - 1)
                last.then_inc(q_done, 1)

            def queries(p, i=0, k=0):
                sA = HD_S + 2 * p
                n = HD_N + 8 * p
                for x in range(4):
                    if x % 2 == 0:
                        wait(pe, lo_ready, sA + x // 2 + 1, i, 2 * k)
                    wait(pe, psum_read, n + x - BANKS + 1, i, 8 * k)
                    blocks3((n + x) % BANKS, sA + x // 2, KQ * (x % 2))

            def latents(p, i=0, k=0):
                sA = HD_S + 2 * p
                n = HD_N + 8 * p
                for e in range(2):
                    wait(pe, qnlo_done, 2 * p + e + 1, i, 2 * k)
                    for c in range(KL):
                        x = 4 + 2 * e + c
                        wait(pe, psum_read, n + x - BANKS + 1, i, 8 * k)
                        w = slice((6 + c) * P, (7 + c) * P)
                        s = (sA + e) % RING
                        passes(ps[:, (n + x) % BANKS, 0:T], whi[:, s, w], wlo[:, s, w], qnhi[:, e, :], qnlo[:, e, :],
                               True, True).then_inc(slab_used if c else q_done, 1)

            def scores(p, i=0, k=0):
                wait(pe, qrlo_done, p + 1, i, k)
                for e in range(2):
                    wait(pe, psum_read, HD_N + 8 * p + 6 + 2 * e, i, 8 * k)
                    wait(pe, sm_done, 2 * p + e - 1, i, 2 * k)
                    for lo, width, q0 in ((0, P, 0), (P, 2 * P, P)):
                        out = ps[:, 4 + e, lo:lo + width]
                        qs = slice(q0, q0 + P)
                        for c in range(KL):
                            passes(out, qlhi[:, e, c, qs], qllo[:, e, c, qs], cThi[:, c, 0:width], cTlo[:, c, 0:width],
                                   c == 0, False)
                        last = passes(out, qrhi[:, qs], qrlo[:, qs], krzhi[:, e, 0:width], krzlo[:, e, 0:width],
                                      False, True)
                    last.then_inc(sc_done, 1)

            def turn(p, i=0, k=0):
                for e in range(2):
                    hd = 2 * p - 2 + e
                    wait(pe, pn_done, 2 * hd + 2, i, 4 * k)
                    wait(pe, olo_done, hd - 1, i, 2 * k)
                    for b in range(3):
                        last = pe.transpose(ps[:, 6 + e, b * P:b * P + P], pr[:, e, b * P:b * P + P], ident[:])
                    last.then_inc(pt_done, 1)

            def attend(p, i=0, k=0):
                for e in range(2):
                    wait(pe, ptlo_done, 2 * p - 1 + e, i, 2 * k)
                    for c in range(KL):
                        w = slice(c * P, c * P + P)
                        passes(ps[:, 6 + e, c * NP_:(c + 1) * NP_], cNhi[:, 0, w], cNlo[:, 0, w], pthi[:, e, 0:NP_],
                               ptlo[:, e, 0:NP_], True, False)
                        last = passes(ps[:, 6 + e, c * NP_ + P:(c + 1) * NP_], cNhi[:, 1, w], cNlo[:, 1, w],
                                      pthi[:, e, NP_:3 * P], ptlo[:, e, NP_:3 * P], False, True)
                    last.then_inc(pv_done, 1)

            pe.wait_ge(c_done, KL)
            for kb in range(2):
                for c in range(KL):
                    last = pe.transpose(ps[:, 6, kb * LAT + c * P:kb * LAT + c * P + P], cT[:, c, kb * P:kb * P + P], ident[:])
            last.then_inc(cn_done, 1)
            for c in range(KL):
                last = pe.transpose(ps[0:NS, 7, c * P:c * P + P], cT[:, c, NP_:T], ident[:])
            last.then_inc(cn_done, 1)
            pe.wait_ge(cqlo_done, KQ)

            def out_of_latent(p, i=0, k=0):
                for e in range(2):
                    hd = 2 * p - 2 + e
                    wait(pe, ollo_done, hd + 1, i, 2 * k)
                    for c in range(KL):
                        last = passes(ps[:, 6 + e, 0:NP_], uvhi[:, 2 * hd + c, :], uvlo[:, 2 * hd + c, :],
                                      olhi[:, e, c, :], ollo[:, e, c, :], c == 0, c == KL - 1)
                    last.then_inc(uv_done, 1)

            queries(0)
            latents(0)
            pe.wait_ge(ctlo_done, 1)
            pe.wait_ge(krlo_done, 2)
            pe.wait_ge(cnlo_done, 1)
            pe.wait_ge(cns_done, 1)
            scores(0)
            pe.wait_ge(uvlo_done, 1)
            for p in range(1, PAIRS):
                queries(p)
                turn(p)
                latents(p)
                attend(p)
                scores(p)
                out_of_latent(p)
            turn(PAIRS)
            attend(PAIRS)
            out_of_latent(PAIRS)

            pe.wait_ge(qs_done, 6 * PAIRS + 1)

            new = slice(NP_, T)
            for c in range(KL):
                pe.matmul(ps[0:NS, 4, 0:NS * H], cT[:, c, new], qsl[:, c].rearrange("p s h -> p (s h)"), start=c == 0,
                          stop=False)
            pe.matmul(ps[0:NS, 4, 0:NS * H], kr[:, new], qsr[:, 0].rearrange("p s h -> p (s h)"), start=False,
                      stop=True).then_inc(snT_done, 1)
            pe.wait_ge(snr_done, 1)
            for s in range(NS):
                last = pe.transpose(ps[0:H, 5, s * NS:(s + 1) * NS], ns_row[:, s * H:(s + 1) * H], ident[0:NS, 0:NS])
            last.then_inc(snt_done, 1)

            def sample_scores(t, i):
                wait(pe, qf_done, 2 * t + 2, i, 4)
                wait(pe, keys_ready[t], 16 * PAGES, i, 16 * PAGES)
                wait(pe, sexp_done, 3 * t - 3, i, 6)
                for b in range(2):
                    g = slice(HALF * b, HALF * b + HALF)
                    out = ps[0:H, 2 * t + b, :].rearrange("p (g k) -> p g k", g=HALF)
                    for c in range(KL):
                        pe.matmul(out, qf[:, t, c, :], kt[:, t, g, c * P:(c + 1) * P], start=c == 0, stop=False)
                    for z in range(2):
                        last = pe.matmul(out[:, :, z * ROPE:(z + 1) * ROPE], qf[:, t, KL + z, :], kt[:, t, g, LAT:KEYT],
                                         start=False, stop=z == 1)
                last.then_inc(ssc_done, 1)

            def turned(out, src, first):
                if first:
                    return pe.matmul(out, src, ident[0:H, 0:H], start=True, stop=True)
                return pe.transpose(out, src, ident[0:H, 0:H])

            def turn_probs(t, i):
                wait(pe, sexp_done, 3 * t + 3, i, 6)
                if isinstance(i, int) and t == 0:
                    pe.wait_ge(nsc_done, 1)
                wait(pe, ptc_done, 2 * t, i, 4)
                for g in range(PAGES):
                    turned(ps[:, 5, g * H:(g + 1) * H], probs[g // HALF][:, g % HALF * P:(g % HALF + 1) * P], g == 0)
                pe.transpose(ps[0:NS, 5, PAGES * H:(PAGES + 1) * H], probs_new, ident[0:H, 0:H]).then_inc(spt_done, 1)

            def sample_attend(t, i):
                o = t % 2
                wait(pe, rows_ready[o], 16 * PAGES * (t // 2 + 1), i, 16 * PAGES)
                wait(pe, ptc_done, 2 * t + 2, i, 4)
                wait(pe, os_done, t, i, 2)
                out = ps[0:H, 6, o * LAT:(o + 1) * LAT]
                for g in range(PAGES):
                    pe.matmul(out, pT[:, g, :], row_of[o][:, g, :], start=g == 0, stop=False)
                pe.matmul(out, pT_new, cNs[:], start=False, stop=True).then_inc(spv_done, 1)

            def turn_out(t, i):
                wait(pe, os_done, t + 1, i, 2)
                for c in range(KL):
                    last = turned(ps[:, 7 - 3 * (t % 2), c * H:(c + 1) * H], os_[t % 2][:, c * P:(c + 1) * P], c == 0)
                last.then_inc(olt_done, 1)

            sample_scores(0, 0)
            sample_scores(1, 0)
            turn_probs(0, 0)
            sample_attend(0, 0)
            with pe.Fori(1, NS // 2) as i:
                for t in range(2):
                    sample_scores(t, i)
                    turn_probs(t - 1, i)
                    turn_out(t - 2, i)
                    sample_attend(t - 1, i)
            turn_probs(NS - 1, 0)
            turn_out(NS - 2, 0)
            sample_attend(NS - 1, 0)
            pe.wait_ge(ols_done, NS - 2)
            turn_out(NS - 1, 0)
            pe.wait_ge(olslo_done, 1)
            for hd in range(H):
                for c in range(KL):
                    last = passes(ps[:, 0, hd * NS:hd * NS + NS], uvhi[:, 2 * hd + c, :], uvlo[:, 2 * hd + c, :],
                                  olshi[:, c, hd, :], olslo[:, c, hd, :], c == 0, c == KL - 1)
            last.then_inc(uvs_done, 1)
            pe.wait_ge(olos_done, 1)

            out_product("wo", 2, KS, lambda b: (ohi[:, b, :], olo[:, b, :]), None)
            ffn(1)
            norm_sum("final")


def _slabs(w, per_chunk):
    K, M = w.shape
    w = w.reshape(K // P, P, M // P, P).transpose(2, 0, 1, 3)
    pad = per_chunk * BLK - w.shape[1]
    if pad:
        w = np.concatenate([w, np.zeros((w.shape[0], pad, P, P), w.dtype)], axis=1)
    return w.reshape(-1, BLK, P, P).transpose(0, 2, 1, 3).reshape(-1, P, SLAB)


def _rope_columns(w):
    half = ROPE // 2
    return w, np.concatenate([w[..., half:], w[..., :half]], axis=-1)


def kernel(**inputs):
    import concourse.bacc as bacc
    from concourse.bass_utils import run_bass_kernel_spmd as run

    x = {k: np.asarray(a) for k, a in inputs.items()}
    f32 = np.float32
    w_in = x["sgu_w_in"][0]
    parts = [_slabs(w_in[:, DS:], 1), _slabs(w_in[:, :DS], 1), _slabs(x["sgu_w_out"][0], 2)]

    def ffn(layer):
        w = x["ffn_w_in"][layer]
        both = np.stack([_slabs(w[:, :FF], 1), _slabs(w[:, FF:], 1)], axis=1)
        return [both.reshape(-1, P, SLAB), _slabs(x["ffn_w_out"][layer], FO)]

    parts += ffn(0)
    parts.append(_slabs(x["w_dq"][0], 1))
    plain, swapped = _rope_columns(x["w_dkv"][:, LAT:])
    parts.append(_slabs(np.concatenate([x["w_dkv"][:, :LAT], plain, plain, swapped, swapped], axis=1), 1))
    w_uq = x["w_uq"][0].reshape(KQ, P, H, NOPE + ROPE)
    plain, swapped = _rope_columns(w_uq[..., NOPE:])
    uk = x["w_uk"].reshape(KL, P, H, NOPE).transpose(2, 0, 3, 1)
    for p in range(PAIRS):
        a, b = 2 * p, 2 * p + 1
        slab_a = [w_uq[:, :, a, :NOPE], w_uq[:, :, b, :NOPE], uk[a]]
        slab_b = [np.concatenate([r[:, :, a], r[:, :, b]], axis=-1) for r in (plain, swapped)] + [uk[b]]
        for s in (slab_a, slab_b):
            parts.append(np.concatenate(s, axis=0).transpose(1, 0, 2).reshape(1, P, SLAB))
    parts.append(_slabs(x["w_o"][0], 2))
    parts += ffn(1)
    w_stream = np.concatenate(parts, axis=0)
    assert w_stream.shape[0] == SLABS

    rows = lambda g: np.ascontiguousarray(g.reshape(-1, P).T)
    gains = np.stack([x["norm_mix"][0], x["norm_mix"][1], x["norm_ffn"][0], x["norm_ffn"][1], x["kv_norm"],
                      x["final_norm"]])
    pos = np.concatenate([np.arange(NP_, dtype=f32), np.full(NS, PAST, f32)])
    inv = (THETA ** (-np.arange(0, ROPE, 2) / ROPE)).astype(f32)
    angle = (pos[None, :] * inv[:, None]).astype(f32)
    cos, sin = np.cos(angle).astype(f32), np.sin(angle).astype(f32)
    arrays = {
        "xT": np.concatenate([x["x_prompt"].reshape(NP_, D), x["x_sample"].reshape(NS, D)]).T,
        "w_stream": w_stream,
        "w_uv": x["w_uv"].reshape(KL, P, H, P).transpose(1, 2, 0, 3).reshape(P, H * KL, P),
        "gains": gains.reshape(6, KD, P).transpose(2, 0, 1).reshape(P, 6 * KD),
        "v_gain": rows(x["sgu_v_norm"][0]),
        "lat_gain": rows(x["kv_latent_norm"]),
        "q_gain": rows(x["q_norm"][0]),
        "wsT": x["sgu_w_s"][0].transpose(2, 0, 1),
        "ws00_in": np.broadcast_to(x["sgu_w_s"][0][:, 0, 0], (P, GROUPS)),
        "bs": np.broadcast_to(x["sgu_b_s"][0].reshape(-1), (P, GROUPS * P)),
        "cosT": np.concatenate([cos] * 4),
        "sinT": np.concatenate([-sin, sin] * 2),
        "keysT": np.concatenate(
            [x["cache_kv_latent"].reshape(PHYS, P, KL, P).transpose(0, 3, 2, 1).reshape(PHYS, P, LAT),
             x["cache_k_rope"].reshape(PHYS, 2, P // 2, ROPE).transpose(0, 1, 3, 2).reshape(PHYS, P, ROPE)], axis=-1),
        "rows": x["cache_kv_latent"],
        "table": x["page_table"].reshape(1, NS * PAGES),
    }
    arrays = {k: np.ascontiguousarray(a) for k, a in arrays.items()}
    outs = {"y_out": (P, KD, T), "c_out": (P, KL, T), "kr_out": (ROPE, T), "v_out": (P, KS, NS)}
    nc = bacc.Bacc("TRN2", target_bir_lowering=False, num_devices=1)
    args = [nc.dram_tensor(k, a.shape, mybir.dt.from_np(a.dtype), kind="ExternalInput").ap() for k, a in arrays.items()]
    args += [nc.dram_tensor(k, shape, F32, kind="ExternalOutput").ap() for k, shape in outs.items()]
    build(nc, *args)
    r = run(nc, [arrays], core_ids=[0]).results[0]

    def tokens(a):
        return np.ascontiguousarray(a.transpose(2, 1, 0).reshape(a.shape[2], -1))

    y, c, v = tokens(r["y_out"]), tokens(r["c_out"]), tokens(r["v_out"])
    krot = np.ascontiguousarray(r["kr_out"].T)
    return (y[:NP_][None], y[NP_:][:, None], c[:NP_][None], krot[:NP_][None], c[NP_:][:, None], krot[NP_:][:, None],
            v[None, :, None])
```

```python
from contextlib import ExitStack

import numpy as np
import concourse.bass as bass
from concourse import mybir

F32 = mybir.dt.float32
F32R = mybir.dt.float32r
I32 = mybir.dt.int32
ACT = mybir.ActivationFunctionType
ALU = mybir.AluOpType
AX = mybir.AxisListType.X

P = 128
D = 1024
NP_, NS = 256, 8
T = NP_ + NS
KD = D // P
DS = 2048
KS = DS // P
GROUPS = 8
FF = 2816
KF = FF // P
H = 16
PAIRS = H // 2
LAT, ROPE, NOPE = 256, 64, 128
KL = LAT // P
QR = 384
KQ = QR // P
PAGES, PHYS = 8, 80
KEYT = LAT + ROPE
HALF = PAGES // 2
SCALE = float((NOPE + ROPE) ** -0.5)
EPS = 1e-6
NEG = -3.0e38
PAST = 1024
THETA = 10000.0

BLK = 8
SLAB = BLK * P
RING = 4
AHEAD = 3
BANKS = 4
FO = 3

STAGES = {}
_s = _n = 0
for _name, _chunks, _slabs in (("v", KS, KS), ("u", KS, KS), ("so", KD, 2 * KD), ("fi0", 2 * KF, 2 * KF),
                               ("fo0", KD, FO * KD), ("dq", KQ, KQ), ("kv", 4, 4), ("hd", 8 * PAIRS, 2 * PAIRS),
                               ("wo", KD, 2 * KD), ("fi1", 2 * KF, 2 * KF), ("fo1", KD, FO * KD)):
    STAGES[_name] = (_s, _n)
    _s += _slabs
    _n += _chunks
SLABS = _s

NORMS = [("mix0", D, KD), ("v", DS, KS), ("ffn0", D, KD), ("mix1", D, KD), ("q", QR, KQ), ("lat", LAT, KL),
         ("ffn1", D, KD), ("final", D, KD)]
NQ = {name: q for q, (name, _, _) in enumerate(NORMS)}
ACC0 = [1 + sum(n + 1 for _, _, n in NORMS[:q]) for q in range(len(NORMS))]
SQ0 = [sum(n for _, _, n in NORMS[:q]) for q in range(len(NORMS))]
STEPS = 4


def wait(eng, sem, c, i=0, k=0):
    if isinstance(i, int):
        if c + k * i > 0:
            eng.wait_ge(sem, c + k * i)
    else:
        eng.wait_ge(sem, i * k + c if k else c)


def build(nc, xT, w_stream, w_uv, gains, v_gain, lat_gain, q_gain, wsT, ws00_in, bs, cosT, sinT, keysT, rows, table,
          y_out, c_out, kr_out, v_out):
    with ExitStack() as ctx:
        def sb(name, shape, dt=F32, c=ctx):
            return c.enter_context(nc.sbuf_tensor(name, shape, dt))

        def sem(name):
            return ctx.enter_context(nc.semaphore(name))

        ps = ctx.enter_context(nc.psum_tensor("ps", [P, 8, 512], F32))

        raw = sb("raw", [P, RING, SLAB])
        whi = sb("whi", [P, RING, SLAB], F32R)
        wlo = sb("wlo", [P, RING, SLAB], F32R)
        h = sb("h", [P, KD, T])
        xhi = sb("xhi", [P, KD, T], F32R)
        xlo = sb("xlo", [P, KD, T], F32R)
        ident = sb("ident", [P, P])
        ones = sb("ones", [P, P])
        Ra = sb("Ra", [P, T])
        Rb = sb("Rb", [P, T])
        Rc = sb("Rc", [P, T])
        ms = sb("ms", [P, T])
        yr = sb("yr", [P, T])
        yy = sb("yy", [P, T])
        acc = sb("acc", [P, T])
        sq = sb("sq", [P, 2, T])
        tt = sb("tt", [P, 3, T])
        eps = sb("eps", [P, 1])
        one = sb("one", [P, 1])
        idle = sb("idle", [P, 2 * len(NORMS) + 1])
        gn = sb("gn", [P, 6, KD, 1])
        gv = sb("gv", [P, KS, 1])
        gl = sb("gl", [P, KL, 1])
        gq = sb("gq", [P, KQ, 1])
        tab = sb("tab", [1, NS * PAGES], I32)
        G = {"mix0": 0, "mix1": 1, "ffn0": 2, "ffn1": 3, "kv": 4, "final": 5}

        cosb = sb("cosb", [P, T])
        sinb = sb("sinb", [P, T])
        mask = sb("mask", [P, 3 * P])
        masks = sb("masks", [H, NS, NS])

        with ExitStack() as a:
            v = sb("v", [P, KS, T], c=a)
            wsraw = sb("wsraw", [P, GROUPS, P], c=a)
            wshi = sb("wshi", [P, GROUPS, P], F32R, a)
            wslo = sb("wslo", [P, GROUPS, P], F32R, a)
            bsb = sb("bsb", [P, GROUPS, P], c=a)
            ws00 = sb("ws00", [P, GROUPS, 1], c=a)
            vn = sb("vn", [P, 2, NP_], c=a)
            vs = sb("vs", [P, KS, NS], c=a)
            vthi = sb("vthi", [P, 2, 2, P], F32R, a)
            vtlo = sb("vtlo", [P, 2, 2, P], F32R, a)
            u = sb("u", [P, 4, T], c=a)
            mb = sb("mb", [P, 2, T], c=a)
            gt = sb("gt", [P, 2, T], c=a)
            ghi = sb("ghi", [P, KS, T], F32R, a)
            glo = sb("glo", [P, KS, T], F32R, a)

        with ExitStack() as f:
            ahi = sb("ahi", [P, KF, T], F32R, f)
            alo = sb("alo", [P, KF, T], F32R, f)

        ohi = sb("ohi", [P, H, T], F32R)
        olo = sb("olo", [P, H, T], F32R)
        cT = sb("cT", [P, KL, T])
        kr = sb("kr", [P, T])
        cThi = sb("cThi", [P, KL, NP_], F32R)
        cTlo = sb("cTlo", [P, KL, NP_], F32R)
        cNs = sb("cNs", [NS, LAT])
        with ExitStack() as n:
            cNhi = sb("cNhi", [P, 2, LAT], F32R, n)
            cNlo = sb("cNlo", [P, 2, LAT], F32R, n)
            krzhi = sb("krzhi", [P, 2, NP_], F32R, n)
            krzlo = sb("krzlo", [P, 2, NP_], F32R, n)
        rows0 = sb("rows0", [P, PAGES, LAT])
        mxh = sb("mxh", [P, 2, 2])
        nmh = sb("nmh", [P, 2, 2])
        rsh = sb("rsh", [P, 2, 2])
        rih = sb("rih", [P, 2, 2])
        uvhi = sb("uvhi", [P, H * KL, P], F32R)
        uvlo = sb("uvlo", [P, H * KL, P], F32R)
        qsl = sb("qsl", [P, KL, NS, H])
        qsr = sb("qsr", [P, 2, NS, H])
        with ExitStack() as b:
            cqhi = sb("cqhi", [P, KQ, T], F32R, b)
            cqlo = sb("cqlo", [P, KQ, T], F32R, b)
            with ExitStack() as b1:
                uvraw = sb("uvraw", [P, H * KL, P], c=b1)
            with ExitStack() as b3:
                x2hi = sb("x2hi", [P, KD, T], F32R, b3)
                x2lo = sb("x2lo", [P, KD, T], F32R, b3)
            with ExitStack() as b2:
                qnhi = sb("qnhi", [P, 2, T], F32R, b2)
                qnlo = sb("qnlo", [P, 2, T], F32R, b2)
                qrhi = sb("qrhi", [P, T], F32R, b2)
                qrlo = sb("qrlo", [P, T], F32R, b2)
                qlhi = sb("qlhi", [P, 2, KL, T], F32R, b2)
                qllo = sb("qllo", [P, 2, KL, T], F32R, b2)
                pr = sb("pr", [P, 2, 3 * P], c=b2)
        pthi = xhi[:, 4:7, :].rearrange("p a b -> p (a b)")[:, 0:6 * P].rearrange("p (e k) -> p e k", e=2)
        ptlo = xlo[:, 4:7, :].rearrange("p a b -> p (a b)")[:, 0:6 * P].rearrange("p (e k) -> p e k", e=2)
        olhi = xhi[:, 0:4, :].rearrange("p a b -> p (a b)")[:, 0:8 * P].rearrange("p (e c k) -> p e c k", e=2, c=KL)
        ollo = xlo[:, 0:4, :].rearrange("p a b -> p (a b)")[:, 0:8 * P].rearrange("p (e c k) -> p e c k", e=2, c=KL)

        kt = sb("kt", [P, 2, PAGES, KEYT])
        rows1 = sb("rows1", [P, PAGES, LAT])
        row_of = (rows0, rows1)
        qf = sb("qf", [P, 2, 4, H])
        nm = sb("nm", [H, 2, 1])
        rs = sb("rs", [H, 2, 3])
        rt = sb("rt", [H, 2, 1])
        ri = sb("ri", [H, 2, 1])
        mxs = sb("mxs", [H, 2, 1])
        mxn = sb("mxn", [H, NS, 1])
        nsc = sb("nsc", [H, NS, NS])
        probs = (sq[0:H].rearrange("p a t -> p (a t)")[:, 0:HALF * P],
                 tt[0:H].rearrange("p a t -> p (a t)")[:, 0:HALF * P])
        probs_new = tt[0:H].rearrange("p a t -> p (a t)")[:, HALF * P:HALF * P + NS]
        pT = yr[:, 0:PAGES * H].rearrange("p (g h) -> p g h", g=PAGES)
        pT_new = yr[0:NS, PAGES * H:(PAGES + 1) * H]
        os_ = (ms[0:H, 0:LAT], yy[0:H, 0:LAT])
        ns_row = tt[0:NS, 2, 0:NS * H]
        ols = Rc[:, 0:NS * KL * H].rearrange("p (s x) -> p s x", s=NS)
        olshi = xhi[:, 7:8, 0:KL * H * NS].rearrange("p a (c h s) -> p (a c) h s", c=KL, h=H)
        olslo = xlo[:, 7:8, 0:KL * H * NS].rearrange("p a (c h s) -> p (a c) h s", c=KL, h=H)

        raw_ready = [sem(f"raw_ready{r}") for r in range(RING)]
        h_in = [sem(f"h_in{q}") for q in range(KD // 2)]
        gains_in, sgu_in, rope_in, uv_in, tab_in = map(sem, ("gains_in", "sgu_in", "rope_in", "uv_in", "tab_in"))
        keys_ready = [sem(f"keys_ready{r}") for r in range(2)]
        rows_ready = [sem(f"rows_ready{r}") for r in range(2)]
        v_saved, ckr_saved, y_saved = map(sem, ("v_saved", "ckr_saved", "y_saved"))
        const_done, wsm_done = map(sem, ("const_done", "wsm_done"))
        hi_ready, lo_ready, slab_used = map(sem, ("hi_ready", "lo_ready", "slab_used"))
        psum_read = sem("psum_read")
        sq_done, acc_done, sum_done, root_done, norm_step, rms_ready = map(
            sem, ("sq_done", "acc_done", "sum_done", "root_done", "norm_step", "rms_ready"))
        xhi_done, xlo_done = map(sem, ("xhi_done", "xlo_done"))
        gelu_done, wshi_done, wslo_done, vn_done, vs_done, vt_done, vthi_done, vtlo_done = map(
            sem, ("gelu_done", "wshi_done", "wslo_done", "vn_done", "vs_done", "vt_done", "vthi_done", "vtlo_done"))
        mix_done, mixr_done, mbs_done, gt_done, ghi_done, glo_done = map(
            sem, ("mix_done", "mixr_done", "mbs_done", "gt_done", "ghi_done", "glo_done"))
        silu_done, act_done, ahi_done, alo_done = map(sem, ("silu_done", "act_done", "ahi_done", "alo_done"))
        cqhi_done, cqlo_done, rope_step, kr_done, krz_done, krhi_done, krlo_done = map(
            sem, ("cqhi_done", "cqlo_done", "rope_step", "kr_done", "krz_done", "krhi_done", "krlo_done"))
        c_done, cthi_done, ctlo_done, cn_done, cnhi_done, cnlo_done, cns_done, rcs_done, uvhi_done, uvlo_done = map(
            sem, ("c_done", "cthi_done", "ctlo_done", "cn_done", "cnhi_done", "cnlo_done", "cns_done", "rcs_done",
                  "uvhi_done", "uvlo_done"))
        q_done, qnhi_done, qnlo_done, qr_done, qrhi_done, qrlo_done, qlhi_done, qs_done = map(
            sem, ("q_done", "qnhi_done", "qnlo_done", "qr_done", "qrhi_done", "qrlo_done", "qlhi_done", "qs_done"))
        sc_done, sm_done, max_done, nm_done, exp_done, ri_done, pn_done, pt_done, pthi_done, ptlo_done = map(
            sem, ("sc_done", "sm_done", "max_done", "nm_done", "exp_done", "ri_done", "pn_done", "pt_done",
                  "pthi_done", "ptlo_done"))
        pv_done, olhi_done, ollo_done, uv_done, ohi_done, olo_done = map(
            sem, ("pv_done", "olhi_done", "ollo_done", "uv_done", "ohi_done", "olo_done"))
        snT_done, snr_done, snt_done, nsc_done, mxn_done, qsr_done, qf_done = map(
            sem, ("snT_done", "snr_done", "snt_done", "nsc_done", "mxn_done", "qsr_done", "qf_done"))
        ssc_done, mxs_done, snm_done, sexp_done, srt_done, sri_done, spt_done, ptc_done, spv_done, os_done = map(
            sem, ("ssc_done", "mxs_done", "snm_done", "sexp_done", "srt_done", "sri_done", "spt_done", "ptc_done",
                  "spv_done", "os_done"))
        olt_done, ols_done, olshi_done, olslo_done = map(sem, ("olt_done", "ols_done", "olshi_done", "olslo_done"))
        uvs_done, ohis_done, olos_done, y_done = map(sem, ("uvs_done", "ohis_done", "olos_done", "y_done"))

        X0 = {"mix0": 0, "ffn0": KD, "mix1": 2 * KD, "ffn1": 4 * KD}
        HD_S, HD_N = STAGES["hd"]

        def pages_of(e, t, i, out, source, ready):
            for g in range(PAGES):
                at = e.value_load(tab[0:1, bass.ds(i * (2 * PAGES) + (t * PAGES + g), 1)], min_val=0, max_val=PHYS - 1)
                e.dma_start(out[:, g, :], source[at]).then_inc(ready, 16)

        block = ctx.enter_context(nc.Block())

        @block.sync
        def _(sp):
            xk = xT.rearrange("(k p) t -> p k t", p=P)

            def load(c, i=0, k=0):
                wait(sp, lo_ready, c - RING + 1, i, k)
                sp.dma_start(raw[:, c % RING, :], w_stream[i * k + c if k else c]).then_inc(raw_ready[c % RING], 16)

            load(0)
            sp.dma_start(gn[:].rearrange("p g k o -> p (g k o)"), gains).then_inc(gains_in, 16)
            sp.dma_start(h[:, 0:2, :], xk[:, 0:2, :]).then_inc(h_in[0], 16)
            for q in range(1, KD // 2):
                sp.dma_start(h[:, 2 * q:2 * q + 2, :], xk[:, 2 * q:2 * q + 2, :]).then_inc(h_in[q], 16)
            for c in range(1, RING):
                load(c)
            sp.dma_start(gv[:].rearrange("p k o -> p (k o)"), v_gain).then_inc(sgu_in, 16)
            sp.dma_start(wsraw[:], wsT).then_inc(sgu_in, 16)
            sp.dma_start(bsb[:].rearrange("p g t -> p (g t)"), bs).then_inc(sgu_in, 16)
            sp.dma_start(ws00[:].rearrange("p g o -> p (g o)"), ws00_in).then_inc(sgu_in, 16)
            sp.dma_start(cosb[:], cosT).then_inc(rope_in, 16)
            sp.dma_start(sinb[:], sinT).then_inc(rope_in, 16)
            sp.dma_start(gl[:].rearrange("p k o -> p (k o)"), lat_gain).then_inc(rope_in, 16)
            sp.dma_start(gq[:].rearrange("p k o -> p (k o)"), q_gain).then_inc(rope_in, 16)
            sp.dma_start(tab[:], table).then_inc(tab_in, 16)
            first = (STAGES["wo"][0] + AHEAD + RING) // RING
            with sp.Fori(1, first) as i:
                for c in range(RING):
                    load(c, i, RING)
            done = first * RING
            for c in range(done, STAGES["wo"][0] + AHEAD + RING - 1):
                load(c)
            done = STAGES["wo"][0] + AHEAD + RING - 1
            sp.wait_ge(tab_in, 16)

            def load_keys(t, i):
                wait(sp, ssc_done, t - 1, i, 2)
                pages_of(sp, t, i, kt[:, t], keysT, keys_ready[t])

            wait(sp, slab_used, STAGES["wo"][0])
            load_keys(0, 0)
            load(done)
            done += 1
            sp.wait_ge(sc_done, H)
            load_keys(1, 0)
            with sp.Fori(1, NS // 2) as i:
                for t in range(2):
                    load_keys(t, i)
            while done % RING:
                load(done)
                done += 1
            with sp.Fori(0, (SLABS - done) // RING) as i:
                for c in range(RING):
                    load(done + c, i, RING)
            for c in range(done + (SLABS - done) // RING * RING, SLABS):
                load(c)
            for m in range(0, KD, 2):
                sp.wait_ge(y_done, m + 2)
                sp.dma_start(y_out[:, m:m + 2, :], h[:, m:m + 2, :]).then_inc(y_saved, 16)
            sp.wait_ge(y_saved, 16 * KD // 2)

        @block.gpsimd
        def _(pool):
            def splits(first, last):
                def one(c, i=0, k=0):
                    wait(pool, hi_ready, c + 1, i, k)
                    pool.tensor_tensor(wlo[:, c % RING, :], raw[:, c % RING, :], whi[:, c % RING, :].bitcast(F32),
                                       ALU.subtract).then_inc(lo_ready, 1)
                n = (last - first) // RING
                if n > 1:
                    with pool.Fori(0, n) as i:
                        for c in range(RING):
                            one(first + c, i, RING)
                    first += n * RING
                for c in range(first, last):
                    one(c)

            pool.memset(ones[:], 1.0).then_inc(const_done, 1)
            pool.memset(eps[:], EPS).then_inc(const_done, 1)
            pool.memset(one[:], 1.0).then_inc(const_done, 1)
            pool.memset(ident[:], 0.0).then_inc(const_done, 1)
            pool.memset(mask[:], 0.0).then_inc(const_done, 1)
            pool.memset(masks[:], 0.0).then_inc(const_done, 1)
            pool.wait_ge(const_done, 6)
            pool.affine_select(out=ident[:], in_=ident[:], compare_op=ALU.not_equal, fill=1.0, base=0,
                               pattern=[[-1, P]], channel_multiplier=1).then_inc(const_done, 1)
            for at in (0, 2 * P):
                pool.affine_select(out=mask[:, at:at + P], in_=mask[:, at:at + P], compare_op=ALU.is_ge, fill=NEG,
                                   base=0, pattern=[[-1, P]], channel_multiplier=1).then_inc(const_done, 1)
            for sign in (1, -1):
                pool.affine_select(out=masks[:], in_=masks[:], compare_op=ALU.is_ge, fill=NEG, base=0,
                                   pattern=[[-sign, NS], [sign, NS]], channel_multiplier=0).then_inc(const_done, 1)
                pool.wait_ge(const_done, 10 if sign == 1 else 11)
            splits(0, AHEAD)
            pool.wait_ge(sgu_in, 64)
            pool.affine_select(out=wsraw[:], in_=wsraw[:], compare_op=ALU.is_ge, fill=0.0, base=0,
                               pattern=[[0, GROUPS], [1, P]], channel_multiplier=-1).then_inc(wsm_done, 1)
            splits(AHEAD, STAGES["so"][0] + AHEAD)
            pool.dma_start(uvraw[:], w_uv).then_inc(uv_in, 16)
            pool.wait_ge(vs_done, KS)
            pool.dma_start(v_out, vs[:]).then_inc(v_saved, 16)
            splits(STAGES["so"][0] + AHEAD, STAGES["dq"][0] + AHEAD)
            splits(STAGES["dq"][0] + AHEAD, HD_S + AHEAD)
            pool.wait_ge(c_done, KL)
            pool.dma_start(c_out, cT[:]).then_inc(ckr_saved, 16)
            pool.wait_ge(kr_done, 1)
            pool.dma_start(kr_out, kr[0:ROPE, :]).then_inc(ckr_saved, 16)
            splits(HD_S + AHEAD, STAGES["wo"][0] + AHEAD)
            pool.wait_ge(tab_in, 16)

            def load_rows(t, i):
                wait(pool, spv_done, t - 1, i, 2)
                pages_of(pool, t, i, row_of[t], rows, rows_ready[t])

            pool.wait_ge(pv_done, H)
            for t in range(2):
                load_rows(t, 0)
            with pool.Fori(1, NS // 2) as i:
                for t in range(2):
                    load_rows(t, i)
            splits(STAGES["wo"][0] + AHEAD, SLABS)
            pool.wait_ge(v_saved, 16)
            pool.wait_ge(ckr_saved, 32)

        @block.scalar
        def _(act):
            def split(c, i=0, k=0):
                if isinstance(i, int) and c + k * i >= SLABS:
                    return
                wait(act, raw_ready[c % RING], 16 * (c // RING + 1), i, 16 * k // RING)
                wait(act, slab_used, c - RING + 1, i, k)
                act.activation(whi[:, c % RING, :], raw[:, c % RING, :], ACT.Copy).then_inc(hi_ready, 1)

            def square(q, m, src, i=0, k=0):
                wait(act, acc_done, ACC0[q] + m - 1, i, k)
                act.activation(sq[:, m % 2, :], src, ACT.Square).then_inc(sq_done, 1)

            tables = iter(range(2 * len(NORMS) + 1))

            def table(function):
                at = next(tables)
                act.activation(idle[:, at:at + 1], one[:], function)

            def root(name, then=None):
                q = NQ[name]
                table(ACT.Sqrt)
                act.wait_ge(sum_done, q + 1)
                wait(act, rms_ready, q)
                act.activation(yr[:], ps[:, 4, 0:T], ACT.Sqrt, bias=eps[:, 0:1],
                               scale=1.0 / NORMS[q][1]).then_inc(root_done, 1)
                if then:
                    table(then)

            def prepare(name, m, i=0, k=0):
                at = i * k + m if k else m
                square(NQ[name], m, h[:, at, :], i, k)
                if name != "final":
                    gained(name, at)

            def gained(name, at):
                act.activation(xhi[:, at, :], h[:, at, :], ACT.Copy,
                               scale=gn[:, G[name], at, :]).then_inc(xhi_done, 1)
                if name == "mix1":
                    act.activation(x2hi[:, at, :], h[:, at, :], ACT.Copy,
                                   scale=gn[:, G["kv"], at, :]).then_inc(xhi_done, 1)

            act.wait_ge(const_done, 4)
            table(ACT.Square)
            act.wait_ge(gains_in, 16)
            split(0)
            for m in range(KD):
                if m % 2 == 0:
                    act.wait_ge(h_in[m // 2], 16)
                prepare("mix0", m)
                if m == 4:
                    split(1)
            split(2)
            split(3)
            root("mix0", ACT.Gelu_apprx_tanh)

            def v_chunk(u_, i):
                if not isinstance(i, int) or u_:
                    split(u_ + AHEAD, i, 4)
                wait(act, psum_read, u_ + 1, i, 4)
                act.activation(v[:, i * 4 + u_, :], tt[:, u_ % 2, :], ACT.Gelu_apprx_tanh).then_inc(gelu_done, 1)

            for u_ in range(4):
                v_chunk(u_, 0)
            with act.Fori(1, KS // 4) as i:
                for u_ in range(4):
                    v_chunk(u_, i)
            act.wait_ge(wsm_done, 1)
            act.activation(wshi[:], wsraw[:], ACT.Copy).then_inc(wshi_done, 1)

            def gate_hi(u_, i):
                wait(act, gt_done, u_ + 1, i, 4)
                act.activation(ghi[:, i * 4 + u_, :], gt[:, u_ % 2, :], ACT.Copy).then_inc(ghi_done, 1)

            def gelu_u(u_, i):
                wait(act, psum_read, KS + u_ + 1, i, 4)
                wait(act, gt_done, u_ - 3, i, 4)
                act.activation(u[:, u_ % 4, :], tt[:, u_ % 2, :], ACT.Gelu_apprx_tanh).then_inc(gelu_done, 1)

            def u_chunk(u_, i, ahead=True):
                wait(act, vt_done, u_ + 1, i, 4)
                wait(act, mix_done, u_ - 1, i, 4)
                act.activation(vthi[:, u_ % 2, :, :].rearrange("p a b -> p (a b)"), ps[:, 5 + u_ % 2, 0:NP_],
                               ACT.Copy).then_inc(vthi_done, 1)
                if ahead:
                    gelu_u(u_ + 2, i)
                    split(KS + u_ + 2 + AHEAD, i, 4)
                if not isinstance(i, int) or u_:
                    gate_hi(u_ - 1, i)

            split(KS + AHEAD)
            gelu_u(0, 0)
            root("v", ACT.Gelu_apprx_tanh)
            split(KS + 1 + AHEAD)
            gelu_u(1, 0)
            for u_ in range(4):
                u_chunk(u_, 0)
            with act.Fori(1, KS // 4 - 1) as i:
                for u_ in range(4):
                    u_chunk(u_, i)
            for u_ in range(KS - 4, KS):
                u_chunk(u_, 0, ahead=u_ + 2 < KS)
            gate_hi(KS - 1, 0)

            def residual(stage, name, per, unroll, n):
                s0, n0 = STAGES[stage]

                def chunk(m, i, k):
                    for z in range(per):
                        split(s0 + per * m + AHEAD + z, i, per * k)
                    wait(act, psum_read, n0 + m + 1, i, k)
                    prepare(name, m, i, k)
                if stage == "fo1":
                    for m in range(KD):
                        chunk(m, 0, 0)
                else:
                    with act.Fori(0, KD // unroll) as i:
                        for m in range(unroll):
                            chunk(m, i, unroll)

            def ffn_in(layer):
                s0, n0 = STAGES[f"fi{layer}"]
                A0 = KF * layer

                def pair(w, i):
                    split(s0 + 2 * w + AHEAD, i, 4)
                    wait(act, psum_read, n0 + 2 * w + 1, i, 4)
                    wait(act, alo_done, A0 + w - 1, i, 2)
                    act.activation(sq[:, w % 2, :], tt[:, w % 2, :], ACT.Silu).then_inc(silu_done, 1)
                    split(s0 + 2 * w + AHEAD + 1, i, 4)
                    wait(act, act_done, A0 + w + 1, i, 2)
                    act.activation(ahi[:, i * 2 + w, :], sq[:, w % 2, :], ACT.Copy).then_inc(ahi_done, 1)

                root(f"ffn{layer}", ACT.Silu)
                if layer == 0:
                    act.wait_ge(v_saved, 16)
                else:
                    act.wait_ge(ckr_saved, 32)
                for w in range(2):
                    pair(w, 0)
                    if layer == 0:
                        act.wait_ge(uv_in, 16)
                        act.activation(uvhi[:, H * w:H * w + H, :], uvraw[:, H * w:H * w + H, :],
                                       ACT.Copy).then_inc(uvhi_done, 1)
                with act.Fori(1, KF // 2) as i:
                    for w in range(2):
                        pair(w, i)

            residual("so", "ffn0", 2, 4, KD)
            ffn_in(0)
            residual("fo0", "mix1", FO, 4, KD)

            s0, n0 = STAGES["dq"]
            root("mix1")
            act.wait_ge(rope_in, 64)
            for d in range(KQ):
                split(s0 + d + AHEAD)
                act.wait_ge(psum_read, n0 + d + 1)
                square(NQ["q"], d, tt[:, d, :])
                act.activation(cqhi[:, d, :], tt[:, d, :], ACT.Copy, scale=gq[:, d, :]).then_inc(cqhi_done, 1)
            s0, n0 = STAGES["kv"]
            for e in range(4):
                split(s0 + e + AHEAD)
                if e == 0:
                    root("q")
                if e < KL:
                    act.wait_ge(psum_read, n0 + e + 1)
                    square(NQ["lat"], e, cT[:, e, :])
            root("lat", ACT.Exp)
            act.wait_ge(c_done, KL)
            act.activation(cThi[:], cT[:, :, 0:NP_], ACT.Copy).then_inc(cthi_done, 1)
            act.wait_ge(kr_done, 1)
            act.wait_ge(krz_done, 4)
            for e in range(2):
                act.activation(krzhi[64 * e:64 * e + 64, e, :], kr[64 * e:64 * e + 64, 0:NP_],
                               ACT.Copy).then_inc(krhi_done, 1)

            def pair(p, i=0, k=0, q=True, back=True, out=True):
                hd = lambda e: 2 * p + e
                n = HD_N + 8 * p
                for e in range(2):
                    if back:
                        wait(act, nm_done, hd(e) - 1, i, 2 * k)
                        for part, (lo, hi_) in enumerate(((0, P), (P, 3 * P))):
                            act.activation(pr[:, e, lo:hi_], pr[:, e, lo:hi_], ACT.Exp, bias=nmh[:, e, part:part + 1],
                                           accum_out=rsh[:, e, part:part + 1]).then_inc(exp_done, 1)
                    if out:
                        wait(act, uv_done, hd(e) - 3, i, 2 * k)
                        act.activation(ohi[:, i * (2 * k) + (hd(e) - 4) if k else hd(e) - 4, 0:NP_], ps[:, 6 + e, 0:NP_],
                                       ACT.Copy).then_inc(ohi_done, 1)
                if q:
                    split(HD_S + 2 * p + AHEAD, i, 2 * k)
                    for e in range(2):
                        wait(act, psum_read, n + e + 1, i, 8 * k)
                        act.activation(qnhi[:, e, :], tt[:, e, :], ACT.Copy).then_inc(qnhi_done, 1)
                if back:
                    for e in range(2):
                        wait(act, pt_done, hd(e) - 1, i, 2 * k)
                        act.activation(pthi[:, e, :], ps[:, 6 + e, 0:3 * P], ACT.Copy).then_inc(pthi_done, 1)
                if q:
                    wait(act, qr_done, p + 1, i, k)
                    act.activation(qrhi[:], sq[:, 1, :], ACT.Copy).then_inc(qrhi_done, 1)
                    for e in range(2):
                        for c in range(KL):
                            if c:
                                wait(act, slab_used, HD_S + 2 * p + e + 1, i, 2 * k)
                            else:
                                wait(act, q_done, 6 * p + 5 + e, i, 6 * k)
                            act.activation(qlhi[:, e, c, :], ps[:, (n + 4 + 2 * e + c) % BANKS, 0:T],
                                           ACT.Copy).then_inc(qlhi_done, 1)
                if back:
                    for e in range(2):
                        wait(act, pv_done, hd(e) - 1, i, 2 * k)
                        act.activation(olhi[:, e].rearrange("p c k -> p (c k)"), ps[:, 6 + e, :],
                                       ACT.Copy).then_inc(olhi_done, 1)
                if q:
                    split(HD_S + 2 * p + AHEAD + 1, i, 2 * k)

            pair(0, back=False, out=False)
            act.wait_ge(cn_done, 2)
            act.activation(cNhi[:].rearrange("p a b -> p (a b)"), ps[:, 6, :], ACT.Copy).then_inc(cnhi_done, 1)
            pair(1, out=False)
            with act.Fori(0, PAIRS // 2 - 1) as i:
                for p in (2, 3):
                    pair(p, i, 2)
            pair(PAIRS, q=False)
            pair(PAIRS + 1, q=False, back=False)

            def by_key(t, i):
                wait(act, spt_done, t + 1, i, 2)
                wait(act, spv_done, t, i, 2)
                act.activation(pT, ps[:, 5, 0:PAGES * H].rearrange("p (g h) -> p g h", g=PAGES),
                               ACT.Copy).then_inc(ptc_done, 1)
                act.activation(pT_new, ps[0:NS, 5, PAGES * H:(PAGES + 1) * H], ACT.Copy).then_inc(ptc_done, 1)

            def exponentials(t, i, back=True):
                if back:
                    by_key(t - 1, i)
                wait(act, snm_done, t + 1, i, 2)
                for half in range(2):
                    act.activation(probs[half], ps[0:H, 2 * t + half, :], ACT.Exp, bias=nm[:, t, :], scale=SCALE,
                                   accum_out=rs[:, t, half:half + 1]).then_inc(sexp_done, 1)
                act.activation(probs_new, nsc[:, i * 2 + t, :], ACT.Exp, bias=nm[:, t, :], scale=SCALE,
                               accum_out=rs[:, t, 2:3]).then_inc(sexp_done, 1)

            def take_out(t, i):
                o = t % 2
                wait(act, olt_done, t + 1, i, 2)
                act.activation(ols[:, i * 2 + t, :], ps[:, 7 - 3 * o, 0:KL * H],
                               ACT.Copy).then_inc(ols_done, 1)

            for t in range(2):
                exponentials(t, 0, back=t > 0)
            with act.Fori(1, NS // 2) as i:
                for t in range(2):
                    exponentials(t, i)
                    take_out(t - 2, i)
            by_key(NS - 1, 0)
            take_out(NS - 2, 0)
            take_out(NS - 1, 0)
            act.wait_ge(ols_done, NS)
            act.activation(olshi, ols.rearrange("p s (c h) -> p c h s", c=KL), ACT.Copy).then_inc(olshi_done, 1)
            act.wait_ge(uvs_done, 1)
            act.activation(ohi[:, :, NP_:T], ps[:, 0, 0:H * NS].rearrange("p (a b) -> p a b", a=H),
                           ACT.Copy).then_inc(ohis_done, 1)

            residual("wo", "ffn1", 2, 4, KD)
            ffn_in(1)
            residual("fo1", "final", FO, 4, KD)
            root("final")

        @block.vector
        def _(dve):
            def lo_of(out, full, hi):
                return dve.tensor_tensor(out, full, hi.bitcast(F32), ALU.subtract)

            def add_square(q, m, i=0, k=0):
                wait(dve, sq_done, SQ0[q] + m + 1, i, k)
                wait(dve, acc_done, ACC0[q] + m, i, k)
                dve.tensor_tensor(acc[:], acc[:], sq[:, m % 2, :], ALU.add).then_inc(acc_done, 1)

            def inverse_root(name, R):
                q = NQ[name]
                dve.wait_ge(root_done, q + 1)
                dve.tensor_scalar(ms[:], ps[:, 4, 0:T], 1.0 / NORMS[q][1], EPS, ALU.mult, ALU.add).then_inc(norm_step, 1)
                dve.reciprocal(yr[:], yr[:]).then_inc(norm_step, 1)
                dve.memset(acc[:], 0.0).then_inc(acc_done, 1)
                dve.wait_ge(norm_step, STEPS * q + 2)
                dve.tensor_tensor(yy[:], yr[:], yr[:], ALU.mult).then_inc(norm_step, 1)
                dve.wait_ge(norm_step, STEPS * q + 3)
                dve.scalar_tensor_tensor(out=yy[:], in0=yy[:], scalar=-0.5, in1=ms[:], op0=ALU.mult,
                                         op1=ALU.mult).then_inc(norm_step, 1)
                dve.wait_ge(norm_step, STEPS * q + 4)
                dve.scalar_tensor_tensor(out=R[:], in0=yy[:], scalar=1.5, in1=yr[:], op0=ALU.add,
                                         op1=ALU.mult).then_inc(rms_ready, 1)
                dve.wait_ge(rms_ready, q + 1)

            def scaled(out, n, R, i=0, k=0, src=None):
                return dve.tensor_tensor(out, ps[:, n % BANKS, 0:T], R[:], ALU.mult).then_inc(psum_read, 1)

            def prepare(name, m, i=0, k=0):
                at = i * k + m if k else m
                add_square(NQ[name], m, i, k)
                if name != "final":
                    gained(name, m, at, i, k)

            def gained(name, m, at, i=0, k=0):
                per = 2 if name == "mix1" else 1
                for z, (gain, hi, lo) in enumerate(((name, xhi, xlo), ("kv", x2hi, x2lo))[:per]):
                    wait(dve, xhi_done, X0[name] + per * m + z + 1, i, per * k)
                    dve.scalar_tensor_tensor(out=lo[:, at, :], in0=h[:, at, :], scalar=gn[:, G[gain], at, :],
                                             in1=hi[:, at, :].bitcast(F32), op0=ALU.mult,
                                             op1=ALU.subtract).then_inc(xlo_done, 1)

            dve.memset(acc[:], 0.0).then_inc(acc_done, 1)
            dve.wait_ge(gains_in, 16)
            for m in range(KD):
                if m % 2 == 0:
                    dve.wait_ge(h_in[m // 2], 16)
                prepare("mix0", m)
            inverse_root("mix0", Ra)

            def v_chunk(u_, i):
                wait(dve, slab_used, u_ + 1, i, 4)
                wait(dve, gelu_done, u_ - 1, i, 4)
                scaled(tt[:, u_ % 2, :], u_, Ra)
                wait(dve, gelu_done, u_ + 1, i, 4)
                dve.tensor_tensor(sq[:, u_ % 2, :], v[:, i * 4 + u_, :], v[:, i * 4 + u_, :],
                                  ALU.mult).then_inc(sq_done, 1)
                add_square(NQ["v"], u_, i, 4)

            for u_ in range(4):
                v_chunk(u_, 0)
            with dve.Fori(1, KS // 4) as i:
                for u_ in range(4):
                    v_chunk(u_, i)
            dve.wait_ge(wshi_done, 1)
            lo_of(wslo[:], wsraw[:], wshi[:]).then_inc(wslo_done, 1)
            dve.wait_ge(sgu_in, 64)

            def norm_v(u_, i):
                at = i * 4 + u_
                wait(dve, vt_done, u_ - 1, i, 4)
                dve.scalar_tensor_tensor(out=vn[:, u_ % 2, :], in0=v[:, at, 0:NP_], scalar=gv[:, at, :],
                                         in1=Rb[:, 0:NP_], op0=ALU.mult, op1=ALU.mult).then_inc(vn_done, 1)
                dve.scalar_tensor_tensor(out=vs[:, at, :], in0=v[:, at, NP_:T], scalar=gv[:, at, :],
                                         in1=Rb[:, NP_:T], op0=ALU.mult, op1=ALU.mult).then_inc(vs_done, 1)

            def gate(u_, i):
                at = i * 4 + u_
                g = (i * 2 + (u_ // 2))
                slot = u_ % 2
                wait(dve, mix_done, u_ + 1, i, 4)
                dve.tensor_tensor(mb[:, slot, 0:NP_].rearrange("p (a t) -> p a t", a=2),
                                  ps[:, 7, 0:NP_].rearrange("p (a t) -> p a t", a=2),
                                  bsb[:, g, :].unsqueeze(1).broadcast_to([P, 2, P]), ALU.add).then_inc(mixr_done, 1)
                wait(dve, vs_done, u_ + 1, i, 4)
                dve.tensor_scalar(mb[:, slot, NP_:T], vs[:, at, :], ws00[:, g, :], bsb[:, g, 0:1],
                                  ALU.mult, ALU.add).then_inc(mbs_done, 1)
                wait(dve, mixr_done, u_ + 1, i, 4)
                wait(dve, mbs_done, u_ + 1, i, 4)
                wait(dve, gelu_done, KS + u_ + 1, i, 4)
                dve.tensor_tensor(gt[:, slot, :], mb[:, slot, :], u[:, u_ % 4, :], ALU.mult).then_inc(gt_done, 1)

            def gate_lo(u_, i):
                at = i * 4 + u_
                slot = u_ % 2
                wait(dve, ghi_done, u_ + 1, i, 4)
                lo_of(glo[:, at, :], gt[:, slot, :], ghi[:, at, :]).then_inc(glo_done, 1)

            def scaled_u(u_, i):
                wait(dve, slab_used, KS + u_ + 1, i, 4)
                wait(dve, gelu_done, KS + u_ - 1, i, 4)
                scaled(tt[:, u_ % 2, :], u_, Ra)

            def u_chunk(u_, i, ahead=2):
                if ahead == 2:
                    scaled_u(u_ + 2, i)
                if ahead:
                    norm_v(u_ + 1, i)
                wait(dve, vthi_done, u_ + 1, i, 4)
                wait(dve, mix_done, u_ - 1, i, 4)
                lo_of(vtlo[:, u_ % 2, :, :].rearrange("p a b -> p (a b)"), ps[:, 5 + u_ % 2, 0:NP_],
                      vthi[:, u_ % 2, :, :].rearrange("p a b -> p (a b)")).then_inc(vtlo_done, 1)
                if not isinstance(i, int) or u_ > 0:
                    gate(u_ - 1, i)
                if not isinstance(i, int) or u_ > 1:
                    gate_lo(u_ - 2, i)

            scaled_u(0, 0)
            inverse_root("v", Rb)
            scaled_u(1, 0)
            norm_v(0, 0)
            for u_ in range(4):
                u_chunk(u_, 0)
            with dve.Fori(1, KS // 4 - 1) as i:
                for u_ in range(4):
                    u_chunk(u_, i)
            for u_ in range(KS - 4, KS):
                u_chunk(u_, 0, min(2, KS - 1 - u_))
            gate_lo(KS - 2, 0)
            gate(KS - 1, 0)
            gate_lo(KS - 1, 0)

            def residual(stage, name, per, unroll):
                s0, n0 = STAGES[stage]

                def chunk(m, i, k):
                    at = i * k + m if k else m
                    wait(dve, slab_used, s0 + per * (m + 1), i, per * k)
                    dve.tensor_tensor(h[:, at, :], ps[:, (n0 + m) % BANKS, 0:T], h[:, at, :],
                                      ALU.add).then_inc(psum_read, 1)
                    prepare(name, m, i, k)
                if stage == "fo1":
                    for m in range(KD):
                        chunk(m, 0, 0)
                else:
                    with dve.Fori(0, KD // unroll) as i:
                        for m in range(unroll):
                            chunk(m, i, unroll)

            def ffn_in(layer):
                s0, n0 = STAGES[f"fi{layer}"]
                A0 = KF * layer

                def pair(w, i):
                    wait(dve, slab_used, s0 + 2 * w + 1, i, 4)
                    wait(dve, silu_done, A0 + w - 1, i, 2)
                    scaled(tt[:, w % 2, :], n0 + 2 * w, Ra)
                    wait(dve, slab_used, s0 + 2 * w + 2, i, 4)
                    scaled(tt[:, 2, :], n0 + 2 * w + 1, Ra)
                    wait(dve, psum_read, n0 + 2 * w + 2, i, 4)
                    wait(dve, silu_done, A0 + w + 1, i, 2)
                    dve.tensor_tensor(sq[:, w % 2, :], sq[:, w % 2, :], tt[:, 2, :], ALU.mult).then_inc(act_done, 1)
                    wait(dve, ahi_done, A0 + w + 1, i, 2)
                    lo_of(alo[:, i * 2 + w, :], sq[:, w % 2, :], ahi[:, i * 2 + w, :]).then_inc(alo_done, 1)

                inverse_root(f"ffn{layer}", Ra)
                if layer == 0:
                    dve.wait_ge(v_saved, 16)
                else:
                    dve.wait_ge(ckr_saved, 32)
                for w in range(2):
                    pair(w, 0)
                    if layer == 0:
                        dve.wait_ge(uvhi_done, w + 1)
                        lo_of(uvlo[:, H * w:H * w + H, :], uvraw[:, H * w:H * w + H, :],
                              uvhi[:, H * w:H * w + H, :]).then_inc(uvlo_done, 1)
                with dve.Fori(1, KF // 2) as i:
                    for w in range(2):
                        pair(w, i)

            residual("so", "ffn0", 2, 4)
            ffn_in(0)
            residual("fo0", "mix1", FO, 4)

            s0, n0 = STAGES["dq"]
            inverse_root("mix1", Ra)
            dve.wait_ge(rope_in, 64)
            for d in range(KQ):
                dve.wait_ge(slab_used, s0 + d + 1)
                scaled(tt[:, d, :], n0 + d, Ra)
                add_square(NQ["q"], d)
                dve.wait_ge(cqhi_done, d + 1)
                dve.scalar_tensor_tensor(out=cqlo[:, d, :], in0=tt[:, d, :], scalar=gq[:, d, :],
                                         in1=cqhi[:, d, :].bitcast(F32), op0=ALU.mult,
                                         op1=ALU.subtract).then_inc(cqlo_done, 1)
            s0, n0 = STAGES["kv"]
            for e in range(2):
                other = slice(64 * (1 - e), 64 * (1 - e) + 64)
                dve.memset(krzhi[other, e, :].bitcast(F32), 0.0).then_inc(krz_done, 1)
                dve.memset(krzlo[other, e, :].bitcast(F32), 0.0).then_inc(krz_done, 1)
            dve.memset(qsr[ROPE:P, 0], 0.0).then_inc(qs_done, 1)
            for e in range(4):
                dve.wait_ge(slab_used, s0 + e + 1)
                if e < KL:
                    scaled(cT[:, e, :], n0 + e, Ra)
                    if e == 0:
                        inverse_root("q", Rb)
                    add_square(NQ["lat"], e)
                else:
                    scaled(tt[:, e - KL, :], n0 + e, Ra)
            inverse_root("lat", Rc)
            for c in range(KL):
                dve.scalar_tensor_tensor(out=cT[:, c, :], in0=cT[:, c, :], scalar=gl[:, c, :], in1=Rc[:],
                                         op0=ALU.mult, op1=ALU.mult).then_inc(c_done, 1)
            dve.wait_ge(psum_read, n0 + 4)
            dve.tensor_tensor(tt[:, 0, :], tt[:, 0, :], cosb[:], ALU.mult).then_inc(rope_step, 1)
            dve.tensor_tensor(tt[:, 1, :], tt[:, 1, :], sinb[:], ALU.mult).then_inc(rope_step, 1)
            dve.wait_ge(rope_step, 2)
            dve.tensor_tensor(kr[:], tt[:, 0, :], tt[:, 1, :], ALU.add).then_inc(kr_done, 1)
            dve.tensor_tensor(cosb[:], Rb[:], cosb[:], ALU.mult).then_inc(rcs_done, 1)
            dve.tensor_tensor(sinb[:], Rb[:], sinb[:], ALU.mult).then_inc(rcs_done, 1)
            dve.wait_ge(cthi_done, 1)
            lo_of(cTlo[:], cT[:, :, 0:NP_], cThi[:]).then_inc(ctlo_done, 1)
            for e in range(2):
                dve.wait_ge(krhi_done, e + 1)
                lo_of(krzlo[64 * e:64 * e + 64, e, :], kr[64 * e:64 * e + 64, 0:NP_],
                      krzhi[64 * e:64 * e + 64, e, :]).then_inc(krlo_done, 1)
            dve.wait_ge(rcs_done, 2)

            def pair(p, i=0, k=0, q=True, back=True, out=True):
                hd = lambda e: 2 * p + e
                n = HD_N + 8 * p
                if back:
                    for e in range(2):
                        wait(dve, sc_done, hd(e) - 1, i, 2 * k)
                        dve.scalar_tensor_tensor(out=pr[:, e, :], in0=ps[:, 4 + e, 0:3 * P], scalar=SCALE, in1=mask[:],
                                                 op0=ALU.mult, op1=ALU.add).then_inc(sm_done, 1)
                        wait(dve, sm_done, hd(e) - 1, i, 2 * k)
                        dve.tensor_reduce(mxh[:, e, 0:1], pr[:, e, 0:P], AX, ALU.max).then_inc(max_done, 1)
                        dve.tensor_reduce(mxh[:, e, 1:2], pr[:, e, P:3 * P], AX, ALU.max).then_inc(max_done, 1)
                        wait(dve, max_done, 2 * hd(e) - 2, i, 4 * k)
                        dve.tensor_scalar(nmh[:, e, :], mxh[:, e, :], -1.0, None, ALU.mult).then_inc(nm_done, 1)
                for e in range(2):
                    if out:
                        wait(dve, ohi_done, hd(e) - 3, i, 2 * k)
                        at = i * (2 * k) + (hd(e) - 4) if k else hd(e) - 4
                        lo_of(olo[:, at, 0:NP_], ps[:, 6 + e, 0:NP_], ohi[:, at, 0:NP_]).then_inc(olo_done, 1)
                    if back:
                        wait(dve, exp_done, 2 * hd(e) - 2, i, 4 * k)
                        dve.reciprocal(rih[:, e, :], rsh[:, e, :]).then_inc(ri_done, 1)
                        wait(dve, ri_done, hd(e) - 1, i, 2 * k)
                        dve.tensor_scalar(pr[:, e, 0:P], pr[:, e, 0:P], rih[:, e, 0:1], None,
                                          ALU.mult).then_inc(pn_done, 1)
                        dve.tensor_scalar(pr[:, e, P:3 * P], pr[:, e, P:3 * P], rih[:, e, 1:2], None,
                                          ALU.mult).then_inc(pn_done, 1)
                if q:
                    for e in range(2):
                        wait(dve, q_done, 6 * p + e + 1, i, 6 * k)
                        scaled(tt[:, e, :], n + e, Rb)
                    for e in range(2):
                        wait(dve, qnhi_done, hd(e) + 1, i, 2 * k)
                        lo_of(qnlo[:, e, :], tt[:, e, :], qnhi[:, e, :]).then_inc(qnlo_done, 1)
                    wait(dve, q_done, 6 * p + 3, i, 6 * k)
                    scaled(tt[:, 2, :], n + 2, cosb)
                    wait(dve, q_done, 6 * p + 4, i, 6 * k)
                    scaled(sq[:, 0, :], n + 3, sinb)
                if back:
                    for e in range(2):
                        wait(dve, pthi_done, hd(e) - 1, i, 2 * k)
                        lo_of(ptlo[:, e, :], ps[:, 6 + e, 0:3 * P], pthi[:, e, :]).then_inc(ptlo_done, 1)
                if q:
                    wait(dve, psum_read, n + 4, i, 8 * k)
                    dve.tensor_tensor(sq[:, 1, :], tt[:, 2, :], sq[:, 0, :], ALU.add).then_inc(qr_done, 1)
                    wait(dve, qrhi_done, p + 1, i, k)
                    lo_of(qrlo[:], sq[:, 1, :], qrhi[:]).then_inc(qrlo_done, 1)
                    for e in range(2):
                        dve.tensor_copy(qsr[0:ROPE, 0, :, i * (2 * k) + hd(e) if k else hd(e)],
                                        sq[64 * e:64 * e + 64, 1, NP_:T]).then_inc(qs_done, 1)
                    for e in range(2):
                        for c in range(KL):
                            bank = (n + 4 + 2 * e + c) % BANKS
                            wait(dve, qlhi_done, 4 * p + 2 * e + c + 1, i, 4 * k)
                            dve.tensor_copy(qsl[:, c, :, i * (2 * k) + hd(e) if k else hd(e)],
                                            ps[:, bank, NP_:T]).then_inc(qs_done, 1)
                            lo_of(qllo[:, e, c, :], ps[:, bank, 0:T], qlhi[:, e, c, :]).then_inc(psum_read, 1)
                if back:
                    for e in range(2):
                        wait(dve, olhi_done, hd(e) - 1, i, 2 * k)
                        lo_of(ollo[:, e].rearrange("p c k -> p (c k)"), ps[:, 6 + e, :],
                              olhi[:, e].rearrange("p c k -> p (c k)")).then_inc(ollo_done, 1)

            pair(0, back=False, out=False)
            dve.wait_ge(cnhi_done, 1)
            lo_of(cNlo[:].rearrange("p a b -> p (a b)"), ps[:, 6, :],
                  cNhi[:].rearrange("p a b -> p (a b)")).then_inc(cnlo_done, 1)
            dve.tensor_copy(cNs[:], ps[0:NS, 7, 0:LAT]).then_inc(cns_done, 1)
            pair(1, out=False)
            with dve.Fori(0, PAIRS // 2 - 1) as i:
                for p in (2, 3):
                    pair(p, i, 2)
            dve.wait_ge(qs_done, 6 * PAIRS + 1)
            dve.memset(qsr[0:ROPE, 1], 0.0).then_inc(qsr_done, 1)
            dve.tensor_copy(qsr[ROPE:P, 1], qsr[0:ROPE, 0]).then_inc(qsr_done, 1)
            dve.wait_ge(snT_done, 1)
            dve.tensor_copy(ns_row, ps[0:NS, 2, 0:NS * H]).then_inc(snr_done, 1)
            pair(PAIRS, q=False)
            dve.wait_ge(snt_done, 1)
            dve.tensor_tensor(nsc[:].rearrange("p a b -> p (a b)"), ps[0:H, 3, 0:NS * NS],
                              masks[:].rearrange("p a b -> p (a b)"), ALU.add).then_inc(nsc_done, 1)
            dve.wait_ge(nsc_done, 1)
            dve.tensor_reduce(mxn[:].rearrange("p a b -> p (a b)"), nsc[:], AX, ALU.max).then_inc(mxn_done, 1)
            dve.wait_ge(mxn_done, 1)
            dve.wait_ge(qsr_done, 2)

            def queries_of(t, i):
                wait(dve, ssc_done, t - 1, i, 2)
                at = i * 2 + t
                dve.tensor_copy(qf[:, t, 0:KL, :], qsl[:, :, at, :]).then_inc(qf_done, 1)
                dve.tensor_copy(qf[:, t, KL:4, :], qsr[:, :, at, :]).then_inc(qf_done, 1)

            def maximum(t, i):
                o = t % 2
                wait(dve, ssc_done, t + 1, i, 2)
                dve.tensor_reduce(mxs[:, o, :], ps[0:H, 2 * o:2 * o + 2, :].rearrange("p b k -> p (b k)"), AX,
                                  ALU.max).then_inc(mxs_done, 1)
                wait(dve, mxs_done, t + 1, i, 2)
                dve.tensor_scalar(nm[:, o, :], mxs[:, o, :], mxn[:, i * 2 + t, :], -SCALE, ALU.max, ALU.mult).then_inc(snm_done, 1)

            def rest(t, i):
                o = t % 2
                wait(dve, spt_done, t + 1, i, 2)
                dve.tensor_reduce(rt[:, o, :], rs[:, o, :], AX, ALU.add).then_inc(srt_done, 1)
                wait(dve, srt_done, t + 1, i, 2)
                dve.reciprocal(ri[:, o, :], rt[:, o, :]).then_inc(sri_done, 1)
                wait(dve, sri_done, t + 1, i, 2)
                wait(dve, spv_done, t + 1, i, 2)
                dve.tensor_scalar(os_[o], ps[0:H, 6, o * LAT:(o + 1) * LAT], ri[:, o, :], None,
                                  ALU.mult).then_inc(os_done, 1)

            queries_of(0, 0)
            queries_of(1, 0)
            pair(PAIRS + 1, q=False, back=False)
            maximum(0, 0)
            with dve.Fori(1, NS // 2) as i:
                queries_of(0, i)
                maximum(-1, i)
                rest(-2, i)
                queries_of(1, i)
                maximum(0, i)
                rest(-1, i)
            maximum(NS - 1, 0)
            rest(NS - 2, 0)
            rest(NS - 1, 0)
            dve.wait_ge(olshi_done, 1)
            lo_of(olslo, ols.rearrange("p s (c h) -> p c h s", c=KL), olshi).then_inc(olslo_done, 1)
            dve.wait_ge(ohis_done, 1)
            lo_of(olo[:, :, NP_:T], ps[:, 0, 0:H * NS].rearrange("p (a b) -> p a b", a=H),
                  ohi[:, :, NP_:T]).then_inc(olos_done, 1)

            residual("wo", "ffn1", 2, 4)
            ffn_in(1)
            residual("fo1", "final", FO, 4)
            inverse_root("final", Ra)
            for m in range(KD):
                dve.scalar_tensor_tensor(out=h[:, m, :], in0=h[:, m, :], scalar=gn[:, G["final"], m, :], in1=Ra[:],
                                         op0=ALU.mult, op1=ALU.mult).then_inc(y_done, 1)

        @block.tensor
        def _(pe):
            def passes(out, whi_, wlo_, mhi, mlo, start, stop):
                pe.matmul(out, whi_, mhi, start=start, stop=False)
                pe.matmul(out, whi_, mlo, start=False, stop=False)
                return pe.matmul(out, wlo_, mhi, start=False, stop=stop)

            def main(c, n, blocks, rhs, i=0, ks=0, kn=0, ready=None, part=None):
                if not part or part[0] == 0:
                    wait(pe, psum_read, n - BANKS + 1, i, kn)
                out = ps[:, n % BANKS, 0:T]
                for b in range(*part or (blocks,)):
                    s, j = c + b // BLK, b % BLK
                    if j == 0:
                        wait(pe, lo_ready, s + 1, i, ks)
                    if ready:
                        ready(b)
                    w = slice(j * P, j * P + P)
                    last = passes(out, whi[:, s % RING, w], wlo[:, s % RING, w], *rhs(b), b == 0, b == blocks - 1)
                    if j == BLK - 1 or b == blocks - 1:
                        last.then_inc(slab_used, 1)

            def norm_sum(name):
                q = NQ[name]
                wait(pe, rms_ready, q)
                pe.wait_ge(acc_done, ACC0[q] + NORMS[q][2])
                pe.matmul(ps[:, 4, 0:T], ones[:], acc[:], start=True, stop=True).then_inc(sum_done, 1)

            x_of = lambda b: (xhi[:, b, :], xlo[:, b, :])

            def x_ready(name, per=1, off=0):
                return lambda b: pe.wait_ge(xlo_done, X0[name] + per * b + off + 1)

            pe.wait_ge(const_done, 11)
            main(0, 0, KD, x_of, ready=x_ready("mix0"))
            main(1, 1, KD, x_of)
            norm_sum("mix0")
            for u_ in range(2, 4):
                main(u_, u_, KD, x_of)
            with pe.Fori(1, KS // 4) as i:
                for u_ in range(4):
                    main(u_, u_, KD, x_of, i, 4, 4)

            def mix(u_, i):
                slot = u_ % 2
                wait(pe, vtlo_done, u_ + 1, i, 4)
                wait(pe, mixr_done, u_, i, 4)
                g = i * 2 + u_ // 2
                for a in range(2):
                    last = passes(ps[:, 7, a * P:a * P + P], vthi[:, slot, a, :], vtlo[:, slot, a, :],
                                  wshi[:, g, :], wslo[:, g, :], True, True)
                last.then_inc(mix_done, 1)

            def u_chunk(u_, i, ahead=True):
                if ahead:
                    main(KS + u_ + 2, KS + u_ + 2, KD, x_of, i, 4, 4)
                wait(pe, vn_done, u_ + 1, i, 4)
                wait(pe, vtlo_done, u_ - 1, i, 4)
                for a in range(2):
                    last = pe.transpose(ps[:, 5 + u_ % 2, a * P:a * P + P], vn[:, u_ % 2, a * P:a * P + P], ident[:])
                last.then_inc(vt_done, 1)
                if not isinstance(i, int) or u_ > 0:
                    mix(u_ - 1, i)

            main(KS, KS, KD, x_of)
            norm_sum("v")
            main(KS + 1, KS + 1, KD, x_of)
            pe.wait_ge(wslo_done, 1)
            for u_ in range(4):
                u_chunk(u_, 0)
            with pe.Fori(1, KS // 4 - 1) as i:
                for u_ in range(4):
                    u_chunk(u_, i)
            for u_ in range(KS - 4, KS - 2):
                u_chunk(u_, 0)
            gated = lambda b: (ghi[:, b, :], glo[:, b, :])
            g_ready = lambda b: pe.wait_ge(glo_done, b + 1)

            def first_of_so(b0, b1):
                main(*STAGES["so"], KS, gated, ready=g_ready, part=(b0, b1))

            u_chunk(KS - 2, 0, False)
            first_of_so(0, 4)
            u_chunk(KS - 1, 0, False)
            first_of_so(4, 9)
            mix(KS - 1, 0)
            first_of_so(9, KS)

            def out_product(stage, per, blocks, rhs, ready, begun=0):
                s0, n0 = STAGES[stage]
                for m in range(begun, 4):
                    main(s0 + per * m, n0 + m, blocks, rhs, ready=ready if m == 0 else None)
                with pe.Fori(1, KD // 4) as i:
                    for m in range(4):
                        main(s0 + per * m, n0 + m, blocks, rhs, i, 4 * per, 4)

            def ffn(layer):
                s0, n0 = STAGES[f"fi{layer}"]
                name = f"ffn{layer}"
                for c in range(4):
                    main(s0 + c, n0 + c, KD, x_of, ready=x_ready(name) if c == 0 else None)
                    if c == 0:
                        norm_sum(name)
                with pe.Fori(1, KF // 2) as i:
                    for c in range(4):
                        main(s0 + c, n0 + c, KD, x_of, i, 4, 4)
                out_product(f"fo{layer}", FO, KF, lambda b: (ahi[:, b, :], alo[:, b, :]),
                            lambda b: pe.wait_ge(alo_done, KF * layer + b + 1))

            out_product("so", 2, KS, gated, None, begun=1)
            ffn(0)

            s0, n0 = STAGES["dq"]
            for d in range(KQ):
                main(s0 + d, n0 + d, KD, x_of, ready=x_ready("mix1", 2) if d == 0 else None)
                if d == 0:
                    norm_sum("mix1")
            s0, n0 = STAGES["kv"]
            for e in range(4):
                main(s0 + e, n0 + e, KD, lambda b: (x2hi[:, b, :], x2lo[:, b, :]),
                     ready=x_ready("mix1", 2, 1) if e == 0 else None)
                if e == 0:
                    norm_sum("q")
            norm_sum("lat")

            def blocks3(bank, slab, j0):
                w = [slice((j0 + b) * P, (j0 + b + 1) * P) for b in range(KQ)]
                for b in range(KQ):
                    last = passes(ps[:, bank, 0:T], whi[:, slab % RING, w[b]], wlo[:, slab % RING, w[b]],
                                  cqhi[:, b, :], cqlo[:, b, :], b == 0, b == KQ - 1)
                last.then_inc(q_done, 1)

            def queries(p, i=0, k=0):
                sA = HD_S + 2 * p
                n = HD_N + 8 * p
                for x in range(4):
                    if x % 2 == 0:
                        wait(pe, lo_ready, sA + x // 2 + 1, i, 2 * k)
                    wait(pe, psum_read, n + x - BANKS + 1, i, 8 * k)
                    blocks3((n + x) % BANKS, sA + x // 2, KQ * (x % 2))

            def latents(p, i=0, k=0):
                sA = HD_S + 2 * p
                n = HD_N + 8 * p
                for e in range(2):
                    wait(pe, qnlo_done, 2 * p + e + 1, i, 2 * k)
                    for c in range(KL):
                        x = 4 + 2 * e + c
                        wait(pe, psum_read, n + x - BANKS + 1, i, 8 * k)
                        w = slice((6 + c) * P, (7 + c) * P)
                        s = (sA + e) % RING
                        passes(ps[:, (n + x) % BANKS, 0:T], whi[:, s, w], wlo[:, s, w], qnhi[:, e, :], qnlo[:, e, :],
                               True, True).then_inc(slab_used if c else q_done, 1)

            def scores(p, i=0, k=0):
                wait(pe, qrlo_done, p + 1, i, k)
                for e in range(2):
                    wait(pe, psum_read, HD_N + 8 * p + 6 + 2 * e, i, 8 * k)
                    wait(pe, sm_done, 2 * p + e - 1, i, 2 * k)
                    for lo, width, q0 in ((0, P, 0), (P, 2 * P, P)):
                        out = ps[:, 4 + e, lo:lo + width]
                        qs = slice(q0, q0 + P)
                        for c in range(KL):
                            passes(out, qlhi[:, e, c, qs], qllo[:, e, c, qs], cThi[:, c, 0:width], cTlo[:, c, 0:width],
                                   c == 0, False)
                        last = passes(out, qrhi[:, qs], qrlo[:, qs], krzhi[:, e, 0:width], krzlo[:, e, 0:width],
                                      False, True)
                    last.then_inc(sc_done, 1)

            def turn(p, i=0, k=0):
                for e in range(2):
                    hd = 2 * p - 2 + e
                    wait(pe, pn_done, 2 * hd + 2, i, 4 * k)
                    wait(pe, olo_done, hd - 1, i, 2 * k)
                    for b in range(3):
                        last = pe.transpose(ps[:, 6 + e, b * P:b * P + P], pr[:, e, b * P:b * P + P], ident[:])
                    last.then_inc(pt_done, 1)

            def attend(p, i=0, k=0):
                for e in range(2):
                    wait(pe, ptlo_done, 2 * p - 1 + e, i, 2 * k)
                    for c in range(KL):
                        w = slice(c * P, c * P + P)
                        passes(ps[:, 6 + e, c * NP_:(c + 1) * NP_], cNhi[:, 0, w], cNlo[:, 0, w], pthi[:, e, 0:NP_],
                               ptlo[:, e, 0:NP_], True, False)
                        last = passes(ps[:, 6 + e, c * NP_ + P:(c + 1) * NP_], cNhi[:, 1, w], cNlo[:, 1, w],
                                      pthi[:, e, NP_:3 * P], ptlo[:, e, NP_:3 * P], False, True)
                    last.then_inc(pv_done, 1)

            pe.wait_ge(cqlo_done, KQ)

            def out_of_latent(p, i=0, k=0):
                if p == 1:
                    pe.wait_ge(uvlo_done, 2)
                for e in range(2):
                    hd = 2 * p - 2 + e
                    wait(pe, ollo_done, hd + 1, i, 2 * k)
                    for c in range(KL):
                        last = passes(ps[:, 6 + e, 0:NP_], uvhi[:, 2 * hd + c, :], uvlo[:, 2 * hd + c, :],
                                      olhi[:, e, c, :], ollo[:, e, c, :], c == 0, c == KL - 1)
                    last.then_inc(uv_done, 1)

            queries(0)
            pe.wait_ge(c_done, KL)
            for kb in range(2):
                for c in range(KL):
                    last = pe.transpose(ps[:, 6, kb * LAT + c * P:kb * LAT + c * P + P], cT[:, c, kb * P:kb * P + P], ident[:])
            last.then_inc(cn_done, 1)
            for c in range(KL):
                last = pe.transpose(ps[0:NS, 7, c * P:c * P + P], cT[:, c, NP_:T], ident[:])
            last.then_inc(cn_done, 1)
            latents(0)
            pe.wait_ge(ctlo_done, 1)
            pe.wait_ge(krlo_done, 2)
            scores(0)
            pe.wait_ge(cnlo_done, 1)
            pe.wait_ge(cns_done, 1)
            def new_scores():
                pe.wait_ge(qs_done, 6 * PAIRS + 1)
                pe.wait_ge(psum_read, HD_N + 8 * PAIRS)
                out = ps[0:NS, 2, 0:NS * H]
                for c in range(KL):
                    pe.matmul(out, cT[:, c, NP_:T], qsl[:, c].rearrange("p s h -> p (s h)"), start=c == 0, stop=False)
                pe.matmul(out, kr[:, NP_:T], qsr[:, 0].rearrange("p s h -> p (s h)"), start=False,
                          stop=True).then_inc(snT_done, 1)

            for p in range(1, PAIRS):
                queries(p)
                turn(p)
                latents(p)
                attend(p)
                if p == PAIRS - 1:
                    new_scores()
                scores(p)
                if p == PAIRS - 1:
                    pe.wait_ge(snr_done, 1)
                    for s in range(NS):
                        last = pe.transpose(ps[0:H, 3, s * NS:(s + 1) * NS], ns_row[:, s * H:(s + 1) * H],
                                            ident[0:NS, 0:NS])
                    last.then_inc(snt_done, 1)
                out_of_latent(p)
            turn(PAIRS)
            attend(PAIRS)
            out_of_latent(PAIRS)

            def sample_scores(t, i):
                wait(pe, qf_done, 2 * t + 2, i, 4)
                wait(pe, keys_ready[t], 16 * PAGES, i, 16 * PAGES)
                wait(pe, sexp_done, 3 * t - 3, i, 6)
                for b in range(2):
                    g = slice(HALF * b, HALF * b + HALF)
                    out = ps[0:H, 2 * t + b, :].rearrange("p (g k) -> p g k", g=HALF)
                    for c in range(KL):
                        pe.matmul(out, qf[:, t, c, :], kt[:, t, g, c * P:(c + 1) * P], start=c == 0, stop=False)
                    for z in range(2):
                        last = pe.matmul(out[:, :, z * ROPE:(z + 1) * ROPE], qf[:, t, KL + z, :], kt[:, t, g, LAT:KEYT],
                                         start=False, stop=z == 1)
                last.then_inc(ssc_done, 1)

            def turned(out, src, first):
                if first:
                    return pe.matmul(out, src, ident[0:H, 0:H], start=True, stop=True)
                return pe.transpose(out, src, ident[0:H, 0:H])

            def turn_probs(t, i):
                wait(pe, sexp_done, 3 * t + 3, i, 6)
                wait(pe, ptc_done, 2 * t, i, 4)
                for g in range(PAGES):
                    turned(ps[:, 5, g * H:(g + 1) * H], probs[g // HALF][:, g % HALF * P:(g % HALF + 1) * P], g == 0)
                pe.transpose(ps[0:NS, 5, PAGES * H:(PAGES + 1) * H], probs_new, ident[0:H, 0:H]).then_inc(spt_done, 1)

            def sample_attend(t, i):
                o = t % 2
                wait(pe, rows_ready[o], 16 * PAGES * (t // 2 + 1), i, 16 * PAGES)
                wait(pe, ptc_done, 2 * t + 2, i, 4)
                wait(pe, os_done, t, i, 2)
                out = ps[0:H, 6, o * LAT:(o + 1) * LAT]
                for g in range(PAGES):
                    pe.matmul(out, pT[:, g, :], row_of[o][:, g, :], start=g == 0, stop=False)
                pe.matmul(out, pT_new, cNs[:], start=False, stop=True).then_inc(spv_done, 1)

            def turn_out(t, i):
                wait(pe, os_done, t + 1, i, 2)
                for c in range(KL):
                    last = turned(ps[:, 7 - 3 * (t % 2), c * H:(c + 1) * H], os_[t % 2][:, c * P:(c + 1) * P], c == 0)
                last.then_inc(olt_done, 1)

            sample_scores(0, 0)
            pe.wait_ge(nsc_done, 1)
            sample_scores(1, 0)
            turn_probs(0, 0)
            sample_attend(0, 0)
            with pe.Fori(1, NS // 2) as i:
                for t in range(2):
                    sample_scores(t, i)
                    turn_probs(t - 1, i)
                    turn_out(t - 2, i)
                    sample_attend(t - 1, i)
            turn_probs(NS - 1, 0)
            turn_out(NS - 2, 0)
            sample_attend(NS - 1, 0)
            pe.wait_ge(ols_done, NS - 2)
            turn_out(NS - 1, 0)
            pe.wait_ge(olslo_done, 1)
            for hd in range(H):
                for c in range(KL):
                    last = passes(ps[:, 0, hd * NS:hd * NS + NS], uvhi[:, 2 * hd + c, :], uvlo[:, 2 * hd + c, :],
                                  olshi[:, c, hd, :], olslo[:, c, hd, :], c == 0, c == KL - 1)
            last.then_inc(uvs_done, 1)
            pe.wait_ge(olos_done, 1)

            out_product("wo", 2, KS, lambda b: (ohi[:, b, :], olo[:, b, :]), None)
            ffn(1)
            norm_sum("final")


def _slabs(w, per_chunk):
    K, M = w.shape
    w = w.reshape(K // P, P, M // P, P).transpose(2, 0, 1, 3)
    pad = per_chunk * BLK - w.shape[1]
    if pad:
        w = np.concatenate([w, np.zeros((w.shape[0], pad, P, P), w.dtype)], axis=1)
    return w.reshape(-1, BLK, P, P).transpose(0, 2, 1, 3).reshape(-1, P, SLAB)


def _rope_columns(w):
    half = ROPE // 2
    return w, np.concatenate([w[..., half:], w[..., :half]], axis=-1)


def kernel(**inputs):
    import concourse.bacc as bacc
    from concourse.bass_utils import run_bass_kernel_spmd as run

    x = {k: np.asarray(a) for k, a in inputs.items()}
    f32 = np.float32
    w_in = x["sgu_w_in"][0]
    parts = [_slabs(w_in[:, DS:], 1), _slabs(w_in[:, :DS], 1), _slabs(x["sgu_w_out"][0], 2)]

    def ffn(layer):
        w = x["ffn_w_in"][layer]
        both = np.stack([_slabs(w[:, :FF], 1), _slabs(w[:, FF:], 1)], axis=1)
        return [both.reshape(-1, P, SLAB), _slabs(x["ffn_w_out"][layer], FO)]

    parts += ffn(0)
    parts.append(_slabs(x["w_dq"][0], 1))
    plain, swapped = _rope_columns(x["w_dkv"][:, LAT:])
    parts.append(_slabs(np.concatenate([x["w_dkv"][:, :LAT], plain, plain, swapped, swapped], axis=1), 1))
    w_uq = x["w_uq"][0].reshape(KQ, P, H, NOPE + ROPE)
    plain, swapped = _rope_columns(w_uq[..., NOPE:])
    uk = x["w_uk"].reshape(KL, P, H, NOPE).transpose(2, 0, 3, 1)
    for p in range(PAIRS):
        a, b = 2 * p, 2 * p + 1
        slab_a = [w_uq[:, :, a, :NOPE], w_uq[:, :, b, :NOPE], uk[a]]
        slab_b = [np.concatenate([r[:, :, a], r[:, :, b]], axis=-1) for r in (plain, swapped)] + [uk[b]]
        for s in (slab_a, slab_b):
            parts.append(np.concatenate(s, axis=0).transpose(1, 0, 2).reshape(1, P, SLAB))
    parts.append(_slabs(x["w_o"][0], 2))
    parts += ffn(1)
    w_stream = np.concatenate(parts, axis=0)
    assert w_stream.shape[0] == SLABS

    rows = lambda g: np.ascontiguousarray(g.reshape(-1, P).T)
    gains = np.stack([x["norm_mix"][0], x["norm_mix"][1], x["norm_ffn"][0], x["norm_ffn"][1], x["kv_norm"],
                      x["final_norm"]])
    pos = np.concatenate([np.arange(NP_, dtype=f32), np.full(NS, PAST, f32)])
    inv = (THETA ** (-np.arange(0, ROPE, 2) / ROPE)).astype(f32)
    angle = (pos[None, :] * inv[:, None]).astype(f32)
    cos, sin = np.cos(angle).astype(f32), np.sin(angle).astype(f32)
    arrays = {
        "xT": np.concatenate([x["x_prompt"].reshape(NP_, D), x["x_sample"].reshape(NS, D)]).T,
        "w_stream": w_stream,
        "w_uv": x["w_uv"].reshape(KL, P, H, P).transpose(1, 2, 0, 3).reshape(P, H * KL, P),
        "gains": gains.reshape(6, KD, P).transpose(2, 0, 1).reshape(P, 6 * KD),
        "v_gain": rows(x["sgu_v_norm"][0]),
        "lat_gain": rows(x["kv_latent_norm"]),
        "q_gain": rows(x["q_norm"][0]),
        "wsT": x["sgu_w_s"][0].transpose(2, 0, 1),
        "ws00_in": np.broadcast_to(x["sgu_w_s"][0][:, 0, 0], (P, GROUPS)),
        "bs": np.broadcast_to(x["sgu_b_s"][0].reshape(-1), (P, GROUPS * P)),
        "cosT": np.concatenate([cos] * 4),
        "sinT": np.concatenate([-sin, sin] * 2),
        "keysT": np.concatenate(
            [x["cache_kv_latent"].reshape(PHYS, P, KL, P).transpose(0, 3, 2, 1).reshape(PHYS, P, LAT),
             x["cache_k_rope"].reshape(PHYS, 2, P // 2, ROPE).transpose(0, 1, 3, 2).reshape(PHYS, P, ROPE)], axis=-1),
        "rows": x["cache_kv_latent"],
        "table": x["page_table"].reshape(1, NS * PAGES),
    }
    arrays = {k: np.ascontiguousarray(a) for k, a in arrays.items()}
    outs = {"y_out": (P, KD, T), "c_out": (P, KL, T), "kr_out": (ROPE, T), "v_out": (P, KS, NS)}
    nc = bacc.Bacc("TRN2", target_bir_lowering=False, num_devices=1)
    args = [nc.dram_tensor(k, a.shape, mybir.dt.from_np(a.dtype), kind="ExternalInput").ap() for k, a in arrays.items()]
    args += [nc.dram_tensor(k, shape, F32, kind="ExternalOutput").ap() for k, shape in outs.items()]
    build(nc, *args)
    r = run(nc, [arrays], core_ids=[0]).results[0]

    def tokens(a):
        return np.ascontiguousarray(a.transpose(2, 1, 0).reshape(a.shape[2], -1))

    y, c, v = tokens(r["y_out"]), tokens(r["c_out"]), tokens(r["v_out"])
    krot = np.ascontiguousarray(r["kr_out"].T)
    return (y[:NP_][None], y[NP_:][:, None], c[:NP_][None], krot[:NP_][None], c[NP_:][:, None], krot[NP_:][:, None],
            v[None, :, None])
```
